# Optimizing a Trainium2 kernel written in Bass

```python
import jax, jax.numpy as jnp
from jax import lax
import numpy as np

D_MODEL = 1024
BATCH = 1
SEQ = 2048
DEPTH = 1
DEC_BATCH = 8
DEC_SEQ = 1
PAST_LEN = 2048
PAGE_SIZE = 128

N_HEADS = 8
QK_NOPE = 128
QK_ROPE = 64
V_DIM = 128
Q_RANK = 256
KV_RANK = 128
ATT_WIDTH = N_HEADS * V_DIM
SOFTMAX_SCALE = (QK_NOPE + QK_ROPE) ** -0.5
ROPE_BASE = 10000.0
Q_BLOCK = 128
NEG_INF = -1e30
POOL_WINDOWS = (2, 4, 8, 16)
N_POOL_GROUPS = 4
POOL_GROUP_DIM = 128
POOL_WIDTH = N_POOL_GROUPS * POOL_GROUP_DIM
POOL_HIST = 15
EPS = 1e-6
OFF_KV = Q_RANK
OFF_KR = OFF_KV + KV_RANK
OFF_ZA = OFF_KR + QK_ROPE
OFF_UP = OFF_ZA + ATT_WIDTH
OFF_ZP = OFF_UP + POOL_WIDTH
OFF_GA = OFF_ZP + POOL_WIDTH
OFF_GP = OFF_GA + D_MODEL
IN_COLS = OFF_GP + D_MODEL
SPLIT_POINTS = (OFF_KV, OFF_KR, OFF_ZA, OFF_UP, OFF_ZP, OFF_GA, OFF_GP)

kernel_name = "mla_pool_gated_hybrid_step"

def rmsnorm(x, g):
    xf = x.astype(jnp.float32)
    y = xf * lax.rsqrt(jnp.mean(xf * xf, axis=-1, keepdims=True) + EPS)
    return (y * g.astype(jnp.float32)).astype(x.dtype)

def rope(x, pos):
    half = QK_ROPE // 2
    inv = ROPE_BASE ** (-jnp.arange(half, dtype=jnp.float32) / half)
    ang = pos.astype(jnp.float32)[:, None] * inv[None, :]
    shape = (1, pos.shape[0]) + (1,) * (x.ndim - 3) + (half,)
    cos = jnp.cos(ang).reshape(shape)
    sin = jnp.sin(ang).reshape(shape)
    xf = x.astype(jnp.float32)
    x1, x2 = xf[..., :half], xf[..., half:]
    return jnp.concatenate([x1 * cos - x2 * sin, x2 * cos + x1 * sin], axis=-1).astype(x.dtype)

def mla_attend(q_abs, q_r, q_pos, ckv, kr, k_pos):
    s = (jnp.einsum('bqhr,bkr->bhqk', q_abs, ckv).astype(jnp.float32)
         + jnp.einsum('bqhp,bkp->bhqk', q_r, kr).astype(jnp.float32)) * SOFTMAX_SCALE
    mask = q_pos[:, None] >= k_pos[None, :]
    s = jnp.where(mask[None, None], s, NEG_INF)
    p = jax.nn.softmax(s, axis=-1).astype(ckv.dtype)
    return jnp.einsum('bhqk,bkr->bqhr', p, ckv)

def blocked_causal_mla(q_abs, q_r, pos, ckv, kr):
    b, L = q_abs.shape[0], q_abs.shape[1]
    nb = L // Q_BLOCK
    qa_b = q_abs.reshape(b, nb, Q_BLOCK, N_HEADS, KV_RANK).swapaxes(0, 1)
    qr_b = q_r.reshape(b, nb, Q_BLOCK, N_HEADS, QK_ROPE).swapaxes(0, 1)
    qp_b = pos.reshape(nb, Q_BLOCK)

    def one_block(args):
        qa, qr, qp = args
        return mla_attend(qa, qr, qp, ckv, kr, pos)

    o = lax.map(one_block, (qa_b, qr_b, qp_b))
    return o.swapaxes(0, 1).reshape(b, L, N_HEADS, KV_RANK)

def pool_mixer(u, hist, pos, w_pool, pool_scale):
    L = u.shape[1]
    u_ext = jnp.concatenate([hist, u], axis=1)
    cs = jnp.cumsum(u_ext.astype(jnp.float32), axis=1)
    cs = jnp.pad(cs, ((0, 0), (1, 0), (0, 0)))
    end = cs[:, POOL_HIST + 1:POOL_HIST + 1 + L]
    groups = []
    for g, w in enumerate(POOL_WINDOWS):
        lo, hi = g * POOL_GROUP_DIM, (g + 1) * POOL_GROUP_DIM
        start = cs[:, POOL_HIST + 1 - w:POOL_HIST + 1 - w + L, lo:hi]
        cnt = jnp.minimum(w, pos + 1).astype(jnp.float32)[None, :, None]
        groups.append((end[..., lo:hi] - start) / cnt)
    pooled = jnp.concatenate(groups, axis=-1) - u.astype(jnp.float32)
    pooled = pooled.astype(u.dtype).reshape(u.shape[0], L, N_POOL_GROUPS, POOL_GROUP_DIM)
    mixed = jnp.einsum('bsgc,gcd->bsgd', pooled, w_pool).reshape(u.shape[0], L, POOL_WIDTH)
    return mixed * pool_scale, u_ext[:, -POOL_HIST:]

def mixer_layer(x, pos0, pool_hist, past_ckv, past_kr,
                g_pre, w_in, g_q, w_uq, g_kv, w_uk, w_uv, w_o_att,
                w_pool, pool_scale, w_o_pool, w_out):
    b, L, _ = x.shape
    h = rmsnorm(x, g_pre)
    z = h @ w_in
    q_lat, kv_lat, k_r, z_att, u_pool, z_pool, g_att, g_pool = jnp.split(z, SPLIT_POINTS, axis=-1)
    pos = pos0 + jnp.arange(L, dtype=jnp.int32)
    q = (rmsnorm(q_lat, g_q) @ w_uq).reshape(b, L, N_HEADS, QK_NOPE + QK_ROPE)
    q_nope = q[..., :QK_NOPE]
    q_r = rope(q[..., QK_NOPE:], pos)
    q_abs = jnp.einsum('bshn,rhn->bshr', q_nope, w_uk)
    ckv_new = rmsnorm(kv_lat, g_kv)
    kr_new = rope(k_r, pos)
    if past_ckv is None:
        o_lat = blocked_causal_mla(q_abs, q_r, pos, ckv_new, kr_new)
    else:
        ckv_all = jnp.concatenate([past_ckv, ckv_new], axis=1)
        kr_all = jnp.concatenate([past_kr, kr_new], axis=1)
        k_pos = jnp.arange(ckv_all.shape[1], dtype=jnp.int32)
        o_lat = mla_attend(q_abs, q_r, pos, ckv_all, kr_all, k_pos)
    o = jnp.einsum('bshr,rhv->bshv', o_lat, w_uv).reshape(b, L, ATT_WIDTH)
    y_att = (o * jax.nn.silu(z_att)) @ w_o_att
    p, pool_state = pool_mixer(u_pool, pool_hist, pos, w_pool, pool_scale)
    y_pool = (p * jax.nn.silu(z_pool)) @ w_o_pool
    merged = jax.nn.sigmoid(g_att) * y_att + jax.nn.sigmoid(g_pool) * y_pool
    x = x + merged @ w_out
    return x, ckv_new, kr_new, pool_state

def setup_inputs(seed: int = 0) -> dict:
    key = jax.random.key(seed)
    ks = jax.random.split(key, 24)
    n_pages = PAST_LEN // PAGE_SIZE
    n_used = DEC_BATCH * n_pages
    n_phys = n_used + n_used // 4

    def nrm(k, shape, scale):
        return jax.random.normal(k, shape, dtype=jnp.float32) * scale

    def gain(k, shape):
        return 1.0 + 0.05 * jax.random.normal(k, shape, dtype=jnp.float32)

    page_table = jax.random.permutation(ks[0], n_phys)[:n_used].reshape(DEC_BATCH, n_pages).astype(jnp.int32)
    return {
        "x_prompt": nrm(ks[1], (BATCH, SEQ, D_MODEL), 1.0),
        "x_sample": nrm(ks[2], (DEC_BATCH, DEC_SEQ, D_MODEL), 1.0),
        "cache_ckv": nrm(ks[3], (DEPTH, n_phys, PAGE_SIZE, KV_RANK), 1.0),
        "cache_krope": nrm(ks[4], (DEPTH, n_phys, PAGE_SIZE, QK_ROPE), 1.0),
        "state_pool": nrm(ks[5], (DEPTH, DEC_BATCH, POOL_HIST, POOL_WIDTH), 1.0),
        "page_table": page_table,
        "g_pre": gain(ks[6], (DEPTH, D_MODEL)),
        "w_in": nrm(ks[7], (DEPTH, D_MODEL, IN_COLS), D_MODEL ** -0.5),
        "g_q": gain(ks[8], (DEPTH, Q_RANK)),
        "w_uq": nrm(ks[9], (DEPTH, Q_RANK, N_HEADS * (QK_NOPE + QK_ROPE)), Q_RANK ** -0.5),
        "g_kv": gain(ks[10], (DEPTH, KV_RANK)),
        "w_uk": nrm(ks[11], (DEPTH, KV_RANK, N_HEADS, QK_NOPE), KV_RANK ** -0.5),
        "w_uv": nrm(ks[12], (DEPTH, KV_RANK, N_HEADS, V_DIM), KV_RANK ** -0.5),
        "w_o_att": nrm(ks[13], (DEPTH, ATT_WIDTH, D_MODEL), ATT_WIDTH ** -0.5),
        "w_pool": nrm(ks[14], (DEPTH, N_POOL_GROUPS, POOL_GROUP_DIM, POOL_GROUP_DIM), POOL_GROUP_DIM ** -0.5),
        "pool_scale": gain(ks[15], (DEPTH, POOL_WIDTH)),
        "w_o_pool": nrm(ks[16], (DEPTH, POOL_WIDTH, D_MODEL), POOL_WIDTH ** -0.5),
        "w_out": nrm(ks[17], (DEPTH, D_MODEL, D_MODEL), D_MODEL ** -0.5),
        "g_final": gain(ks[18], (D_MODEL,)),
    }

def reference(x_prompt, x_sample, cache_ckv, cache_krope, state_pool, page_table,
              g_pre, w_in, g_q, w_uq, g_kv, w_uk, w_uv, w_o_att,
              w_pool, pool_scale, w_o_pool, w_out, g_final):
    dec_b = x_sample.shape[0]
    past_len = page_table.shape[1] * cache_ckv.shape[2]
    xp, xs = x_prompt, x_sample
    ckv_p, kr_p, pool_p, ckv_s, kr_s, pool_s = [], [], [], [], [], []
    for l in range(DEPTH):
        lw = (g_pre[l], w_in[l], g_q[l], w_uq[l], g_kv[l], w_uk[l], w_uv[l], w_o_att[l],
              w_pool[l], pool_scale[l], w_o_pool[l], w_out[l])
        hist0 = jnp.zeros((xp.shape[0], POOL_HIST, POOL_WIDTH), dtype=xp.dtype)
        xp, c_p, k_p, s_p = mixer_layer(xp, 0, hist0, None, None, *lw)
        past_ckv = cache_ckv[l][page_table].reshape(dec_b, past_len, KV_RANK)
        past_kr = cache_krope[l][page_table].reshape(dec_b, past_len, QK_ROPE)
        xs, c_s, k_s, s_s = mixer_layer(xs, past_len, state_pool[l], past_ckv, past_kr, *lw)
        ckv_p.append(c_p); kr_p.append(k_p); pool_p.append(s_p)
        ckv_s.append(c_s); kr_s.append(k_s); pool_s.append(s_s)
    y_prompt = rmsnorm(xp, g_final)
    y_sample = rmsnorm(xs, g_final)
    return (y_prompt, y_sample, jnp.stack(ckv_p), jnp.stack(kr_p), jnp.stack(pool_p),
            jnp.stack(ckv_s), jnp.stack(kr_s), jnp.stack(pool_s))


_drawn_inputs = setup_inputs


def setup_inputs(seed=0):
    import zlib

    import numpy as np

    out = dict(_drawn_inputs(seed))
    spreads = {}
    factors = {'cache_ckv': 5.279, 'cache_krope': 8.0, 'g_q': 8.0, 'pool_scale': 4.223}
    for name, (base, spread) in spreads.items():
        noise = np.random.default_rng([zlib.crc32(name.encode()), seed]).standard_normal(out[name].shape)
        drawn = base * np.exp(spread * noise) if base else spread * noise
        out[name] = __import__('jax').numpy.asarray(drawn.astype(out[name].dtype))
    for name, factor in factors.items():
        out[name] = (out[name] * factor).astype(out[name].dtype)
    return out
```

```python
from contextlib import ExitStack

import numpy as np
import concourse.bass as bass
from concourse import mybir

f32 = mybir.dt.float32
f32r = mybir.dt.float32r
i32 = mybir.dt.int32
ALU = mybir.AluOpType
ACT = mybir.ActivationFunctionType
AX = mybir.AxisListType

P = 128
D = 1024
KD = D // P
SEQ = 2048
NDEC = 8
NH = 8
NOPE = 128
ROPE = 64
R = 128
QR = 256
KQ = QR // P
PAST = 2048
PAGE = 128
NPAGES = PAST // PAGE
NPHYS = NDEC * NPAGES + NDEC * NPAGES // 4
NG = 4
HIST = 15
WINDOWS = (2, 4, 8, 16)
EPS = 1e-6
SCALE = float((NOPE + ROPE) ** -0.5)
NEG = -1e30

PT = SEQ // P
NT = PT + 1
ROWS = NT * P
LAT = QR + R + ROPE
ABS = NH * R
QROPE = NH * ROPE
QCOLS = QROPE + ABS

HG = 4
NGRP = NH // HG

T = 412
NC = -(-(SEQ + NDEC) // T)
TOK = NC * T
SUB = T // 4
TAIL = 23
LAST = SEQ - (NC - 1) * T


def split(e, low, source, high):
    return e.tensor_tensor(low, source, high.bitcast(f32), ALU.subtract)


def wait(e, sem, value):
    if not isinstance(value, int) or value > 0:
        e.wait_ge(sem, value)


def wait_all(e, known, count, *waits):
    held, counts = [], []
    for sem, value in waits:
        if not isinstance(value, int):
            register = e.alloc_register()
            e.reg_mov(register, value)
            held.append(register)
            value = register
        if not isinstance(value, int) or value > 0:
            counts.append((sem, value))
    e.wait_ge(known, count)
    for sem, value in counts:
        e.wait_ge(sem, value)
    for register in held:
        e.free_register(register)


def three_products(pe, out, stationary, moving, depth, first=True, last=True):
    for k in range(depth):
        for a, b in ((0, 0), (0, 1), (1, 0)):
            mm = pe.matmul(out, stationary(a, k), moving(b, k),
                           start=first and k == 0 and a + b == 0,
                           stop=last and k == depth - 1 and a == 1)
    return mm


def project(nc, io, keep):
    with ExitStack() as ctx:
        def sb(name, shape, dt=f32):
            return ctx.enter_context(nc.sbuf_tensor("a_" + name, shape, dt))

        def sem(name):
            return ctx.enter_context(nc.semaphore("a_" + name))

        ident, kt, kv, mask = keep["ident"], keep["kt"], keep["kv"], keep["mask"]
        ps = [ctx.enter_context(nc.psum_tensor(f"a_ps{n}", [P, 512], f32)) for n in range(8)]
        ps_x, ps_lat, ps_norm, ps_q = ps[0:2], ps[2], ps[3], ps[4:7]

        wlat = sb("wlat", [P, 2, KD, LAT], f32r)
        wq = sb("wq", [P, 2, KQ, QCOLS], f32r)
        gpre = sb("gpre", [P, D])
        gkv = sb("gkv", [P, R])
        gq = sb("gq", [P, KQ])
        cos = sb("cos", [P, NT, ROPE])
        sin = sb("sin", [P, NT, ROPE])
        half = sb("half", [P, 2])
        wlat_f = sb("wlat_f", [P, KD, LAT])
        wq_f = sb("wq_f", [P, KQ, QCOLS])
        wuq_t = sb("wuq_t", [P, NH, QR])
        wuk_t = sb("wuk_t", [P, NH, R])

        x = sb("x", [P, 2, D])
        junk = sb("junk", [P, D])
        h = sb("h", [P, D])
        hf = sb("hf", [P, KD, P])
        ht = sb("ht", [P, 2, KD, P], f32r)
        lat = sb("lat", [P, LAT])
        norm = sb("norm", [P, QR + R + 2 * ROPE])
        qt = sb("qt", [P, 2, KQ, P], f32r)
        qabs = sb("qabs", [P, ABS])
        qrot = sb("qrot", [P, NH, ROPE])
        qcos = sb("qcos", [P, NH, ROPE])
        qsin = sb("qsin", [P, NH, ROPE])
        kcos = sb("kcos", [P, ROPE])
        ksin = sb("ksin", [P, ROPE])
        qout = sb("qout", [P, NH + NH // 2, P])
        stat = sb("stat", [P, 12])
        x_ss, x_var, x_rinv = stat[:, 0:1], stat[:, 1:2], stat[:, 2:3]
        l_ss, l_var, l_rinv = stat[:, 4:6], stat[:, 6:8], stat[:, 8:10]
        C0 = QR
        K0 = QR + R
        H2 = ROPE // 2

        const_in, wlat_in, wq_in = sem("const_in"), sem("wlat_in"), sem("wq_in")
        CONSTS = 16 * 7
        half_ok, absorbed, gq_on, wq_hi, weights_ok = (
            sem("half_ok"), sem("absorbed"), sem("gq_on"), sem("wq_hi"), sem("weights_ok"))
        x_in, x_sq, x_rinv_ok, h_ok = sem("x_in"), sem("x_sq"), sem("x_rinv_ok"), sem("h_ok")
        xt_ok, hf_ok, h_out, ht_ok = sem("xt_ok"), sem("hf_ok"), sem("h_out"), sem("ht_ok")
        lat_ok, lat_sb, lat_sq, rinv_ok = sem("lat_ok"), sem("lat_sb"), sem("lat_sq"), sem("rinv_ok")
        ckv_ok, qn_ok, kr_ok, ckv_out, kr_out = (
            sem("ckv_ok"), sem("qn_ok"), sem("kr_ok"), sem("ckv_out"), sem("kr_out"))
        nt_ok, nt_hi, nt_lo = sem("nt_ok"), sem("nt_hi"), sem("nt_lo")
        q_ok, qabs_ok, qrot_ok = sem("q_ok"), sem("qabs_ok"), sem("qrot_ok")
        qt_ok, qout_a, qout_d, q_out = sem("qt_ok"), sem("qout_a"), sem("qout_d"), sem("q_out")
        dve_done, pool_done, kv_hi = sem("dve_done"), sem("pool_done"), sem("kv_hi")
        ht_hi, qcos_ok, ksq_ok, kro_ok = sem("ht_hi"), sem("qcos_ok"), sem("ksq_ok"), sem("kro_ok")
        var_ok = sem("var_ok")
        lvar_ok = sem("lvar_ok")

        def steps(e, step):
            step(0, True, False, False, False)
            step(1, True, True, False, False)
            step(2, True, True, True, False)
            with e.Fori(3, NT) as i:
                step(i, True, True, True, True)
            step(NT, False, True, True, True)
            step(NT + 1, False, False, True, True)
            step(NT + 2, False, False, False, True)

        block = ctx.enter_context(nc.Block())

        @block.sync
        def _(sp):
            sp.dma_start(ident[:, :], io["ident"]).then_inc(const_in, 16)
            sp.dma_start(gpre[:, :], io["g_pre"].partition_broadcast(P)).then_inc(const_in, 16)
            sp.dma_start(gkv[:, :], io["g_kv"].partition_broadcast(P)).then_inc(const_in, 16)
            sp.dma_start(gq[:, :], io["g_q"]).then_inc(const_in, 16)
            sp.dma_start(cos[:, :, :], io["cos"]).then_inc(const_in, 16)
            sp.dma_start(sin[:, :, :], io["sin"]).then_inc(const_in, 16)
            sp.dma_start(mask[:, :], io["mask"]).then_inc(const_in, 16)

            def step(i, pre, new, mid, old):
                if pre:
                    wait_all(sp, const_in, CONSTS,
                             (h_ok, i - 1),
                             (x_in, 16 * i))
                    sp.dma_start(x[:, bass.ds(i % 2, 1), :], io["x"][bass.ds(i * P, P), :]).then_inc(x_in, 16)
                if new:
                    n = i - 1
                    wait_all(sp, const_in, CONSTS,
                             (hf_ok, 2 * n + 2))
                    sp.dma_start(io["ht"][:, :, bass.ds(n * P, P)], hf[:, :, :]).then_inc(h_out, 16)
                if old:
                    o = i - 3
                    wait_all(sp, const_in, CONSTS,
                             (qout_a, 2 * o + 2),
                             (qout_d, o + 1))
                    sp.dma_start(io["q"][bass.ds(o, 1), :, :, :].rearrange("a p h t -> p (a h) t"),
                                 qout[:, :, :]).then_inc(q_out, 16)
                if new:
                    wait_all(sp, const_in, CONSTS,
                             (ckv_ok, n + 1))
                    sp.dma_start(io["ckv"][bass.ds(n * P, P), :], norm[:, C0:K0]).then_inc(ckv_out, 16)
                    wait_all(sp, const_in, CONSTS,
                             (kr_ok, n + 1))
                    sp.dma_start(io["krope"][bass.ds(n * P, P), :], norm[:, K0:K0 + ROPE]).then_inc(kr_out, 16)

            steps(sp, step)
            for s in (h_out, q_out, ckv_out, kr_out):
                sp.wait_ge(s, 16 * NT)

        @block.gpsimd
        def _(pool):
            pool.memset(half[:, :], -0.5).then_inc(half_ok, 1)
            pool.wait_ge(half_ok, 1)
            pool.wait_ge(const_in, CONSTS)

            def step(i, pre, new, mid, old):
                if pre:
                    wait_all(pool, const_in, CONSTS,
                             (x_sq, i + 1),
                             (h_ok, i))
                    pool.tensor_scalar(x_var, x_ss, 1.0 / D, EPS, ALU.mult, ALU.add).then_inc(var_ok, 1)
                    wait(pool, var_ok, i + 1)
                    pool.tensor_tensor(x_rinv, x_var, half[:, 0:1], ALU.pow).then_inc(x_rinv_ok, 1)
                if new:
                    n = i - 1
                    wait_all(pool, const_in, CONSTS,
                             (lat_sq, 2 * n + 2),
                             (qn_ok, n),
                             (ckv_ok, n))
                    pool.tensor_scalar(l_var[:, 0:1], l_ss[:, 0:1], 1.0 / QR, EPS, ALU.mult, ALU.add)
                    pool.tensor_scalar(l_var[:, 1:2], l_ss[:, 1:2], 1.0 / R, EPS, ALU.mult, ALU.add).then_inc(lvar_ok, 1)
                    wait(pool, lvar_ok, n + 1)
                    pool.tensor_tensor(l_rinv, l_var, half[:, :], ALU.pow).then_inc(rinv_ok, 1)
                    tile_cos = cos[:, bass.ds(n, 1), :].rearrange("p a c -> p (a c)")
                    tile_sin = sin[:, bass.ds(n, 1), :].rearrange("p a c -> p (a c)")
                    wait(pool, kro_ok, n)
                    pool.tensor_tensor(kcos[:, :], lat[:, K0:K0 + ROPE], tile_cos, ALU.mult)
                    pool.tensor_tensor(ksin[:, :], lat[:, K0:K0 + ROPE], tile_sin, ALU.mult).then_inc(ksq_ok, 1)
                    wait(pool, ksq_ok, n + 1)
                    wait(pool, nt_ok, n)
                    wait(pool, kr_out, 16 * n)
                    pool.tensor_tensor(norm[:, K0:K0 + H2], kcos[:, 0:H2], ksin[:, H2:ROPE], ALU.subtract)
                    pool.tensor_tensor(norm[:, K0 + H2:K0 + ROPE], kcos[:, H2:ROPE], ksin[:, 0:H2],
                                       ALU.add).then_inc(kro_ok, 1)
                    wait_all(pool, const_in, CONSTS,
                             (kro_ok, n + 1))
                    pool.tensor_copy(norm[:, K0 + ROPE:K0 + 2 * ROPE], norm[:, K0:K0 + ROPE]).then_inc(kr_ok, 1)

            steps(pool, step)

        @block.scalar
        def _(act):
            act.dma_start(wlat_f[:, :, :], io["w_lat"]).then_inc(wlat_in, 16)
            act.dma_start(wuq_t[:, :, :], io["w_uq_t"]).then_inc(wq_in, 16)
            act.dma_start(wuk_t[:, :, :], io["w_uk_t"]).then_inc(wq_in, 16)
            act.dma_start(wq_f[:, :, 0:QROPE], io["w_uq_rope"]).then_inc(wq_in, 16)
            act.wait_ge(wlat_in, 16)
            act.activation(wlat[:, 0, :, :], wlat_f[:, :, :], ACT.Copy).then_inc(wq_hi, 1)

            def step(i, pre, new, mid, old):
                if new:
                    n = i - 1
                    wait(act, h_out, 16 * n)
                    wait(act, ht_ok, n)
                    for a in range(2):
                        wait(act, xt_ok, 2 * n + 1 + a)
                        act.activation(hf[:, 4 * a:4 * a + 4, :], ps_x[a][:, :], ACT.Copy).then_inc(hf_ok, 1)
                if mid:
                    m = i - 2
                    wait(act, nt_ok, m + 1)
                    act.activation(qt[:, 0, :, :], ps_norm[:, 0:QR], ACT.Copy).then_inc(nt_hi, 1)
                    act.activation(kt[:, bass.ds(m, 1), 0:2, :].rearrange("p a b t -> p (a b t)"),
                                   ps_norm[:, QR:512], ACT.Copy).then_inc(nt_hi, 1)
                if old:
                    o = i - 3
                    wait(act, q_out, 16 * o)
                    for a in range(2):
                        wait(act, qt_ok, 3 * o + 1 + a)
                        act.activation(qout[:, 4 * a:4 * a + 4, :], ps_q[a][:, :], ACT.Copy).then_inc(qout_a, 1)
                if pre:
                    wait(act, x_in, 16 * i + 16)
                    wait(act, x_rinv_ok, i)
                    act.activation(junk[:, :], x[:, bass.ds(i % 2, 1), :].rearrange("p a d -> p (a d)"),
                                   ACT.Square, accum_out=x_ss).then_inc(x_sq, 1)
                if new:
                    wait(act, lat_ok, n + 1)
                    wait(act, ckv_ok, n)
                    wait(act, kro_ok, n)
                    act.activation(lat[:, :], ps_lat[:, 0:LAT], ACT.Copy).then_inc(lat_sb, 1)
                    wait(act, lat_sb, n + 1)
                    act.activation(junk[:, 0:QR], lat[:, 0:QR], ACT.Square, accum_out=l_ss[:, 0:1]).then_inc(lat_sq, 1)
                    act.activation(junk[:, QR:K0], lat[:, C0:K0], ACT.Square, accum_out=l_ss[:, 1:2]).then_inc(lat_sq, 1)
                if mid:
                    wait(act, qt_ok, 3 * m)
                    for a in range(2):
                        wait(act, q_ok, 3 * m + 2 + a)
                        act.activation(qabs[:, 512 * a:512 * a + 512], ps_q[a][:, :], ACT.Copy).then_inc(qabs_ok, 1)
                if new:
                    wait(act, rinv_ok, n + 1)
                    wait(act, nt_ok, n)
                    act.activation(norm[:, 0:QR], lat[:, 0:QR], ACT.Copy, scale=l_rinv[:, 0:1]).then_inc(qn_ok, 1)

            steps(act, step)

        @block.vector
        def _(dve):
            done = [0]

            def own(instruction):
                done[0] += 1
                instruction.then_inc(dve_done, 1)
                dve.wait_ge(dve_done, done[0])

            dve.wait_ge(wq_hi, 1)
            split(dve, wlat[:, 1, :, :], wlat_f[:, :, :], wlat[:, 0, :, :]).then_inc(weights_ok, 1)
            dve.wait_ge(wq_in, 48)
            dve.wait_ge(const_in, CONSTS)
            for k in range(KQ):
                own(dve.tensor_scalar(wq_f[:, k, 0:QROPE], wq_f[:, k, 0:QROPE], gq[:, k:k + 1], None, ALU.mult))
                for a in range(2):
                    dve.wait_ge(absorbed, 2 * k + a + 1)
                    own(dve.tensor_scalar(wq_f[:, k, QROPE + 512 * a:QROPE + 512 * a + 512], ps[4 + 2 * a + k][:, :],
                                          gq[:, k:k + 1], None, ALU.mult))
            own(dve.tensor_copy(wq[:, 0, :, :], wq_f[:, :, :]))
            split(dve, wq[:, 1, :, :], wq_f[:, :, :], wq[:, 0, :, :]).then_inc(weights_ok, 1)

            def step(i, pre, new, mid, old):
                if new:
                    n = i - 1
                    wait(dve, hf_ok, 2 * n + 2)
                    wait(dve, lat_ok, n)
                    dve.tensor_copy(ht[:, 0, :, :], hf[:, :, :]).then_inc(ht_hi, 1)
                    wait(dve, ht_hi, n + 1)
                    split(dve, ht[:, 1, :, :], hf[:, :, :], ht[:, 0, :, :]).then_inc(ht_ok, 1)
                if mid:
                    m = i - 2
                    wait(dve, nt_hi, 2 * m + 2)
                    split(dve, qt[:, 1, :, :].rearrange("p k t -> p (k t)"), ps_norm[:, 0:QR],
                          qt[:, 0, :, :].rearrange("p k t -> p (k t)"))
                    split(dve, kt[:, bass.ds(m, 1), 2:4, :].rearrange("p a b t -> p (a b t)"), ps_norm[:, QR:512],
                          kt[:, bass.ds(m, 1), 0:2, :].rearrange("p a b t -> p (a b t)")).then_inc(nt_lo, 1)
                if old:
                    o = i - 3
                    wait(dve, qt_ok, 3 * o + 3)
                    wait(dve, q_out, 16 * o)
                    dve.tensor_copy(qout[:, NH:NH + NH // 2, :], ps_q[2][:, :]).then_inc(qout_d, 1)
                if pre:
                    wait(dve, x_rinv_ok, i + 1)
                    wait(dve, xt_ok, 2 * i)
                    dve.scalar_tensor_tensor(out=h[:, :], in0=x[:, bass.ds(i % 2, 1), :].rearrange("p a d -> p (a d)"),
                                             scalar=x_rinv, in1=gpre[:, :], op0=ALU.mult, op1=ALU.mult).then_inc(h_ok, 1)
                if mid:
                    tile_cos = cos[:, bass.ds(m, 1), :].to_broadcast([P, NH, ROPE])
                    tile_sin = sin[:, bass.ds(m, 1), :].to_broadcast([P, NH, ROPE])
                    wait(dve, q_ok, 3 * m + 1)
                    wait(dve, qt_ok, 3 * m)
                    q_rope = ps_q[2][:, :].rearrange("p (h c) -> p h c", h=NH)
                    dve.tensor_tensor(qcos[:, :, :], q_rope, tile_cos, ALU.mult)
                    dve.tensor_tensor(qsin[:, :, :], q_rope, tile_sin, ALU.mult).then_inc(qcos_ok, 1)
                    wait(dve, qcos_ok, m + 1)
                    dve.tensor_tensor(qrot[:, :, 0:H2], qcos[:, :, 0:H2], qsin[:, :, H2:ROPE], ALU.subtract)
                    dve.tensor_tensor(qrot[:, :, H2:ROPE], qcos[:, :, H2:ROPE], qsin[:, :, 0:H2], ALU.add).then_inc(qrot_ok, 1)
                if new:
                    wait(dve, rinv_ok, n + 1)
                    wait(dve, nt_ok, n)
                    wait(dve, ckv_out, 16 * n)
                    dve.scalar_tensor_tensor(out=norm[:, C0:K0], in0=lat[:, C0:K0], scalar=l_rinv[:, 1:2],
                                             in1=gkv[:, :], op0=ALU.mult, op1=ALU.mult).then_inc(ckv_ok, 1)
                    wait(dve, ckv_ok, n + 1)
                    high = kv[:, bass.ds(n, 1), 0, :].rearrange("p a r -> p (a r)")
                    dve.tensor_copy(high, norm[:, C0:K0]).then_inc(kv_hi, 1)
                    wait(dve, kv_hi, n + 1)
                    split(dve, kv[:, bass.ds(n, 1), 1, :].rearrange("p a r -> p (a r)"), norm[:, C0:K0],
                          high).then_inc(dve_done, 1)

            steps(dve, step)

        @block.tensor
        def _(pe):
            pe.wait_ge(wq_in, 48)
            for k in range(KQ):
                for a in range(2):
                    for hh in range(4):
                        head = 4 * a + hh
                        mm = pe.matmul(ps[4 + 2 * a + k][:, hh * R:hh * R + R], wuq_t[:, head, k * P:k * P + P],
                                       wuk_t[:, head, :], start=True, stop=True)
                    mm.then_inc(absorbed, 1)
            pe.wait_ge(const_in, CONSTS)
            pe.wait_ge(weights_ok, 2)

            def step(i, pre, new, mid, old):
                if new:
                    n = i - 1
                    wait(pe, h_ok, n + 1)
                    wait(pe, hf_ok, 2 * n)
                    for k in range(KD):
                        mm = pe.transpose(ps_x[k // 4][:, k % 4 * P:k % 4 * P + P], h[:, k * P:k * P + P], ident[:, :])
                        if k % 4 == 3:
                            mm.then_inc(xt_ok, 1)
                if mid:
                    m = i - 2
                    wait(pe, qn_ok, m + 1)
                    wait(pe, ckv_ok, m + 1)
                    wait(pe, kr_ok, m + 1)
                    wait(pe, nt_lo, m)
                    for k in range(4):
                        mm = pe.transpose(ps_norm[:, k * P:k * P + P], norm[:, k * P:k * P + P], ident[:, :])
                    mm.then_inc(nt_ok, 1)
                if old:
                    o = i - 3
                    for a in range(2):
                        wait(pe, qabs_ok, 2 * o + 2)
                        for hh in range(4):
                            c = (4 * a + hh) * R
                            mm = pe.transpose(ps_q[a][:, hh * P:hh * P + P], qabs[:, c:c + R], ident[:, :])
                        mm.then_inc(qt_ok, 1)
                    wait(pe, qrot_ok, o + 1)
                    for hh in range(NH // 2):
                        mm = pe.transpose(ps_q[2][:, hh * P:hh * P + P],
                                          qrot[:, 2 * hh:2 * hh + 2, :].rearrange("p h c -> p (h c)"), ident[:, :])
                    mm.then_inc(qt_ok, 1)
                if new:
                    wait(pe, ht_ok, n + 1)
                    wait(pe, lat_sb, n)
                    three_products(pe, ps_lat[:, 0:LAT], lambda a, k: ht[:, a, k, :],
                                   lambda b, k: wlat[:, b, k, :], KD).then_inc(lat_ok, 1)
                if mid:
                    wait(pe, nt_lo, m + 1)
                    for group, columns in ((2, 0), (0, QROPE), (1, QROPE + 512)):
                        if group == 2:
                            wait(pe, qout_d, m)
                        else:
                            wait(pe, qout_a, 2 * m)
                        three_products(pe, ps_q[group][:, :], lambda a, k: qt[:, a, k, :],
                                       lambda b, k: wq[:, b, k, columns:columns + 512], KQ).then_inc(q_ok, 1)

            steps(pe, step)


def attend_steps():
    units = PT * NGRP
    out = []
    for u in range(units + 1):
        scores, products = [], []
        if u < units:
            chunks = -(-(u // NGRP + 1) // 4)
            for h in range(HG):
                scores += [("S", u, h, c) for c in range(chunks)]
        if u > 0:
            tiles = (u - 1) // NGRP + 1
            products = [("T", u - 1, 0)]
            for j in range(tiles):
                if j + 1 < tiles:
                    products.append(("T", u - 1, j + 1))
                products.append(("V", u - 1, j))
        lead = min(len(scores), 2)
        placed = 0
        for k in range(max(1, len(scores))):
            if k < len(scores):
                out.append(scores[k])
            if k + 1 >= lead:
                share = len(products) * (k + 2 - lead) // max(1, len(scores) + 1 - lead)
                out += products[placed:share]
                placed = share
        out += products[placed:]
    steps, due = [], []
    for step in out:
        if step[0] == "T" and step[2] == 0:
            steps += [p for _, p in due]
            due = []
        while due and due[0][0] <= 0:
            steps.append(due.pop(0)[1])
        steps.append(step)
        due = [(n - 1, p) for n, p in due]
        if step[0] == "S" and step[3] == -(-(step[1] // NGRP + 1) // 4) - 1:
            due.append((1, ("P", step[1], step[2])))
    return steps


def attend(nc, io, keep):
    with ExitStack() as ctx:
        def sb(name, shape, dt=f32):
            return ctx.enter_context(nc.sbuf_tensor("b_" + name, shape, dt))

        def sem(name):
            return ctx.enter_context(nc.semaphore("b_" + name))

        ident, kt, kv, mask = keep["ident"], keep["kt"], keep["kv"], keep["mask"]
        ps = [ctx.enter_context(nc.psum_tensor(f"b_ps{n}", [P, 512], f32)) for n in range(8)]
        NS, NTB, NPT = 4, 2, 3
        ps_s, ps_t, ps_o = ps[0:NS], ps[NS:NS + NTB], ps[6:8]
        qf = [sb(f"qf{n}", [P, 2, HG, P]) for n in range(2)]
        qs = [sb(f"qs{n}", [P, 3, HG, P], f32r) for n in range(2)]
        sp_ = [sb(f"p{n}", [P, SEQ]) for n in range(2 * HG)]
        pt = [sb(f"pt{n}", [P, 2, HG * P], f32r) for n in range(NPT)]
        ol = [sb(f"ol{n}", [P, HG * P]) for n in range(2)]
        top = sb("top", [P, 2 * HG, 4])
        low = sb("low", [P, 2 * HG, 4])
        bias = sb("bias", [P, 2 * HG])
        total = sb("total", [P, 2 * HG])
        inverse = sb("inverse", [P, 2 * HG])

        q_in = [sem("q_in0"), sem("q_in1")]
        q_hi, q_half, q_ok = sem("q_hi"), sem("q_half"), sem("q_ok")
        s_ok, s_sb, bias_ok, exp_ok, inv_ok, p_ok = (
            sem("s_ok"), sem("s_sb"), sem("bias_ok"), sem("exp_ok"), sem("inv_ok"), sem("p_ok"))
        t_ok, pt_hi, pt_ok, v_ok, ol_ok = sem("t_ok"), sem("pt_hi"), sem("pt_ok"), sem("v_ok"), sem("ol_ok")
        o_out = [sem("o_out0"), sem("o_out1")]

        steps = attend_steps()
        units = PT * NGRP
        number = {}
        for kind in "SPTV":
            for n, step in enumerate(x for x in steps if x[0] == kind):
                number[step] = n
        tiles = lambda u: u // NGRP + 1
        chunks = lambda u: -(-tiles(u) // 4)
        last_turn = lambda u: number["T", u, tiles(u) - 1] + 1
        last_product = lambda u: number["V", u, tiles(u) - 1] + 1
        first_score = lambda step: step[0] == "S" and step[2] == 0 and step[3] == 0
        last_score = lambda step: step[0] == "S" and step[3] == chunks(step[1]) - 1

        block = ctx.enter_context(nc.Block())

        @block.sync
        def _(sp):
            def load_q(u):
                i, g = u // NGRP, u % NGRP
                if u >= 2:
                    sp.wait_ge(q_hi, 2 * (u - 1))
                    sp.wait_ge(q_ok, u - 1)
                at = 2 * HG
                sp.dma_start(qf[u % 2][:, 0, :, :], io["q"][i, :, HG * g:HG * g + HG, :]).then_inc(q_in[u % 2], 16)
                for half in range(2):
                    pairs = io["q"][i, ROPE * half:ROPE * half + ROPE, at + 2 * g:at + 2 * g + 2, :]
                    for copy in range(2):
                        sp.dma_start(qf[u % 2][ROPE * copy:ROPE * copy + ROPE, 1, half:HG:2, :],
                                     pairs).then_inc(q_in[u % 2], 16)

            load_q(0)
            load_q(1)
            for u in range(units):
                if u + 2 < units:
                    load_q(u + 2)
                i, g = u // NGRP, u % NGRP
                sp.wait_ge(ol_ok, u + 1)
                sp.dma_start(io["olat"][:, HG * g:HG * g + HG, i * P:i * P + P],
                             ol[u % 2][:, :].rearrange("p (h t) -> p h t", h=HG)).then_inc(o_out[u % 2], 16)
            for n in range(2):
                sp.wait_ge(o_out[n], 16 * units // 2)

        @block.gpsimd
        def _(pool):
            for u in range(units):
                pool.wait_ge(q_in[u % 2], 80 * (u // 2 + 1))
                pool.wait_ge(q_hi, 2 * (u + 1))
                if u >= 1:
                    pool.wait_ge(q_ok, u)
                split(pool, qs[u % 2][:, 1, :, :], qf[u % 2][:, 0, :, :], qs[u % 2][:, 0, :, :]).then_inc(q_half, 1)
                pool.wait_ge(q_half, u + 1)
                split(pool, qs[u % 2][ROPE:P, 2, :, :], qf[u % 2][ROPE:P, 1, :, :],
                      qs[u % 2][ROPE:P, 2, :, :]).then_inc(q_ok, 1)

        @block.scalar
        def _(act):
            def split_q(u):
                act.wait_ge(q_in[u % 2], 80 * (u // 2 + 1))
                if u >= 2:
                    act.wait_ge(s_ok, number["S", u - 2, HG - 1, chunks(u - 2) - 1] + 1)
                act.activation(qs[u % 2][:, 0, :, :], qf[u % 2][:, 0, :, :], ACT.Copy).then_inc(q_hi, 1)
                act.activation(qs[u % 2][:, 2, :, :], qf[u % 2][:, 1, :, :], ACT.Copy).then_inc(q_hi, 1)

            split_q(0)
            for step in steps:
                u = step[1]
                if first_score(step) and u + 1 < units:
                    split_q(u + 1)
                if last_score(step):
                    h = step[2]
                    row = (u % 2) * HG + h
                    keys = tiles(u) * P
                    act.wait_ge(bias_ok, HG * u + h + 1)
                    act.activation(sp_[row][:, 0:keys], sp_[row][:, 0:keys], ACT.Exp, bias=bias[:, row:row + 1],
                                   scale=SCALE, accum_out=total[:, row:row + 1]).then_inc(exp_ok, 1)
                elif step[0] == "T":
                    n = number[step]
                    act.wait_ge(t_ok, n + 1)
                    if n >= NPT:
                        act.wait_ge(v_ok, n - NPT + 1)
                    act.activation(pt[n % NPT][:, 0, :], ps_t[n % NTB][:, :], ACT.Copy).then_inc(pt_hi, 1)
                elif step[0] == "V" and step[2] == tiles(u) - 1:
                    act.wait_ge(v_ok, last_product(u))
                    if u >= 2:
                        act.wait_ge(o_out[u % 2], 16 * (u // 2))
                    act.activation(ol[u % 2][:, :], ps_o[u % 2][:, :], ACT.Copy).then_inc(ol_ok, 1)

        @block.vector
        def _(dve):
            for step in steps:
                u = step[1]
                if step[0] == "S":
                    _, _, h, c = step
                    row = (u % 2) * HG + h
                    n = number[step]
                    keys = min(4, tiles(u) - 4 * c) * P
                    dve.wait_ge(s_ok, n + 1)
                    if u >= 2 and c == 0:
                        dve.wait_ge(t_ok, last_turn(u - 2))
                    out, inp = sp_[row][:, 512 * c:512 * c + keys], ps_s[n % NS][:, 0:keys]
                    if c == chunks(u) - 1:
                        dve.tensor_tensor_reduce(out=out, in0=inp, in1=mask[:, 512 - keys:512], scale=1.0,
                                                 scalar=3 * NEG, op0=ALU.add, op1=ALU.max,
                                                 accum_out=top[:, row, c:c + 1]).then_inc(s_sb, 1)
                    else:
                        dve.tensor_scalar(out, inp, 1.0, None, ALU.mult, ALU.max,
                                          accum_out=top[:, row, c:c + 1]).then_inc(s_sb, 1)
                    if c == chunks(u) - 1:
                        dve.wait_ge(s_sb, n + 1)
                        if u >= 2:
                            dve.wait_ge(exp_ok, HG * (u - 2) + h + 1)
                        dve.tensor_scalar(low[:, row, 0:chunks(u)], top[:, row, 0:chunks(u)], -SCALE, None, ALU.mult,
                                          ALU.min, accum_out=bias[:, row:row + 1]).then_inc(bias_ok, 1)
                elif step[0] == "P":
                    h = step[2]
                    row = (u % 2) * HG + h
                    keys = tiles(u) * P
                    dve.wait_ge(exp_ok, HG * u + h + 1)
                    dve.reciprocal(inverse[:, row:row + 1], total[:, row:row + 1]).then_inc(inv_ok, 1)
                    dve.wait_ge(inv_ok, HG * u + h + 1)
                    dve.tensor_scalar(sp_[row][:, 0:keys], sp_[row][:, 0:keys], inverse[:, row:row + 1], None,
                                      ALU.mult).then_inc(p_ok, 1)
                elif step[0] == "T":
                    n = number[step]
                    dve.wait_ge(pt_hi, n + 1)
                    split(dve, pt[n % NPT][:, 1, :], ps_t[n % NTB][:, :], pt[n % NPT][:, 0, :]).then_inc(pt_ok, 1)

        @block.tensor
        def _(pe):
            for step in steps:
                u = step[1]
                if step[0] == "S":
                    _, _, h, c = step
                    n = number[step]
                    first, keys = 4 * c, min(4, tiles(u) - 4 * c)
                    if h == 0 and c == 0:
                        pe.wait_ge(q_ok, u + 1)
                    if n >= NS:
                        pe.wait_ge(s_sb, n - NS + 1)
                    q = qs[u % 2]
                    pairs = ((0, 0), (0, 2), (1, 0), (2, 1), (2, 3))
                    for k, (a, b) in enumerate(pairs):
                        mm = pe.matmul(ps_s[n % NS][:, 0:keys * P], q[:, a, h, :], kt[:, first:first + keys, b, :],
                                       start=k == 0, stop=k == len(pairs) - 1)
                    mm.then_inc(s_ok, 1)
                elif step[0] == "T":
                    j, n = step[2], number[step]
                    if j == 0:
                        pe.wait_ge(p_ok, HG * (u + 1))
                    if n >= NTB:
                        pe.wait_ge(pt_ok, n - NTB + 1)
                    for h in range(HG):
                        mm = pe.transpose(ps_t[n % NTB][:, h * P:h * P + P],
                                          sp_[(u % 2) * HG + h][:, j * P:j * P + P], ident[:, :])
                    mm.then_inc(t_ok, 1)
                elif step[0] == "V":
                    j, n = step[2], number[step]
                    pe.wait_ge(pt_ok, n + 1)
                    if j == 0 and u >= 2:
                        pe.wait_ge(ol_ok, u - 1)
                    for k, (a, b) in enumerate(((0, 0), (0, 1), (1, 0))):
                        mm = pe.matmul(ps_o[u % 2][:, :], kv[:, j, a, :], pt[n % NPT][:, b, :],
                                       start=j == 0 and k == 0, stop=j == tiles(u) - 1 and k == 2)
                    mm.then_inc(v_ok, 1)


def decode(nc, io, keep):
    with ExitStack() as ctx:
        def sb(name, shape, dt=f32):
            return ctx.enter_context(nc.sbuf_tensor("c_" + name, shape, dt))

        def sem(name):
            return ctx.enter_context(nc.semaphore("c_" + name))

        ident, kt = keep["ident"], keep["kt"]
        bank = [ctx.enter_context(nc.psum_tensor(f"c_ps{n}", [P, 512], f32)) for n in range(8)]
        ps_c, ps_r, ps_s, ps_new, ps_o = bank[0:2], bank[2:4], bank[4:8], bank[2], bank[3]
        SH = NDEC * NH
        ROW = SH + NH
        RUN = PAST // P
        PARTS = ((0, 0), (0, 1), (1, 0))
        STEPS = NDEC * 4
        pages = sb("pages", [P, NDEC], i32)
        part = sb("part", [P, NDEC], i32)
        rows = sb("rows", [P, NDEC], i32)
        cn = [sb(f"cn{s}", [P, RUN, R]) for s in range(NDEC)]
        rn = [sb(f"rn{s}", [P, RUN, ROPE]) for s in range(NDEC)]
        cnew = sb("cnew", [NDEC, R])
        q = sb("q", [P, 3, NH, NDEC])
        qc_f = sb("qc_f", [P, 3, SH])
        qp_f = sb("qp_f", [P, 3, NDEC * ROW])
        qc = sb("qc", [P, 2, 3, SH], f32r)
        qp = sb("qp", [P, 2, 3, NDEC * ROW], f32r)
        ckeys = [sb(f"ckeys{n}", [P, 2, 4, P], f32r) for n in range(2)]
        rkeys = [sb(f"rkeys{n}", [P, 2, 2, P], f32r) for n in range(2)]
        own = sb("own", [SH, NDEC])
        sc = sb("sc", [SH, PAST + NDEC])
        pt = sb("pt", [P, RUN, SH])
        ptn = sb("ptn", [NDEC, SH])
        o = sb("o", [NH, NDEC, R])
        top = sb("top", [SH, 5])
        low = sb("low", [SH, 5])
        stat = sb("stat", [SH, 3])
        bias, total, inverse = stat[:, 0:1], stat[:, 1:2], stat[:, 2:3]
        olat = sb("olat", [P, NH, TOK - SEQ])

        pages_in, rows_ok, q_in, new_in = sem("pages_in"), sem("rows_ok"), sem("q_in"), sem("new_in")
        cache_in = [sem(f"cache_in{s}") for s in range(NDEC)]
        q_zero, qc_f_ok, qp_f_ok, q_hi, q_ok = (
            sem("q_zero"), sem("qc_f_ok"), sem("qp_f_ok"), sem("q_hi"), sem("q_ok"))
        turned, keys_hi, keys_ok, s_ok, new_ok = (
            sem("turned"), sem("keys_hi"), sem("keys_ok"), sem("s_ok"), sem("new_ok"))
        s_sb, bias_ok, exp_ok, inv_ok, p_ok = sem("s_sb"), sem("bias_ok"), sem("exp_ok"), sem("inv_ok"), sem("p_ok")
        o_sb, o_turned = sem("o_sb"), sem("o_turned")
        pt_turned, pt_ok, o_ok, olat_ok, olat_out = (
            sem("pt_turned"), sem("pt_ok"), sem("o_ok"), sem("olat_ok"), sem("olat_out"))

        block = ctx.enter_context(nc.Block())

        @block.sync
        def _(sp):
            sp.dma_start(pages[:, :], io["pages"]).then_inc(pages_in, 16)
            sp.dma_start(part[:, :], io["page_part"]).then_inc(pages_in, 16)
            sp.wait_ge(q_zero, 1)
            sp.dma_start(q[:, 0, :, :], io["q"][NT - 1, :, 0:NH, 0:NDEC]).then_inc(q_in, 16)
            for half in range(2):
                for copy in range(2):
                    sp.dma_start(q[ROPE * copy:ROPE * copy + ROPE, 1 + copy, half:NH:2, :],
                                 io["q"][NT - 1, ROPE * half:ROPE * half + ROPE, NH:NH + NH // 2, 0:NDEC]
                                 ).then_inc(q_in, 16)
            sp.dma_start(own[:, :], io["own"]).then_inc(new_in, 16)
            sp.dma_start(cnew[:, :], io["ckv"][SEQ:SEQ + NDEC, :]).then_inc(new_in, 16)
            sp.wait_ge(olat_ok, 2)
            sp.dma_start(io["olat"][:, :, SEQ:TOK], olat[:, :, :]).then_inc(olat_out, 16)
            sp.wait_ge(olat_out, 16)

        @block.gpsimd
        def _(pool):
            pool.wait_ge(rows_ok, 1)
            for s in range(NDEC):
                at = bass.IndirectOffsetOnAxis(ap=rows[:, s:s + 1], axis=0)
                pool.indirect_dma_start(cn[s][:, :, :].rearrange("p t r -> p (t r)"), None, io["cache_ckv"],
                                        at).then_inc(cache_in[s], 16)
                pool.indirect_dma_start(rn[s][:, :, :].rearrange("p t r -> p (t r)"), None, io["cache_krope"],
                                        at).then_inc(cache_in[s], 16)

        @block.scalar
        def _(act):
            act.wait_ge(qp_f_ok, 1)
            act.activation(qp[:, 0, :, :], qp_f[:, :, :], ACT.Copy).then_inc(q_hi, 1)
            act.activation(qc[:, 0, :, :], qc_f[:, :, :], ACT.Copy).then_inc(q_hi, 1)
            for n in range(STEPS):
                act.wait_ge(turned, n + 1)
                if n >= 2:
                    act.wait_ge(s_ok, n - 1)
                act.activation(ckeys[n % 2][:, 0, :, :], ps_c[n % 2][:, :], ACT.Copy).then_inc(keys_hi, 1)
                act.activation(rkeys[n % 2][:, 0, :, :], ps_r[n % 2][:, 0:2 * P], ACT.Copy).then_inc(keys_hi, 1)
            act.wait_ge(bias_ok, 1)
            act.activation(sc[:, :], sc[:, :], ACT.Exp, bias=bias, scale=SCALE, accum_out=total).then_inc(exp_ok, 1)
            act.wait_ge(pt_turned, 1)
            act.activation(pt[:, 0:RUN // 2, :], bank[0][:, :], ACT.Copy).then_inc(pt_ok, 1)
            act.wait_ge(pt_turned, 3)
            act.activation(ptn[:, :], ps_new[0:NDEC, 0:SH], ACT.Copy).then_inc(pt_ok, 1)
            for n in range(2):
                act.wait_ge(o_ok, n + 1)
                act.activation(o[:, 4 * n:4 * n + 4, :], ps_s[n][0:NH, :], ACT.Copy).then_inc(o_sb, 1)
            act.wait_ge(o_turned, 1)
            act.activation(olat[:, :, 0:NDEC].rearrange("p h s -> p s h"),
                           ps_o[:, 0:SH].rearrange("p (s h) -> p s h", s=NDEC), ACT.Copy).then_inc(olat_ok, 1)

        @block.vector
        def _(dve):
            dve.wait_ge(pages_in, 32)
            dve.scalar_tensor_tensor(rows[:, :], pages[:, :], PAGE // RUN, part[:, :], ALU.mult,
                                     ALU.add).then_inc(rows_ok, 1)
            dve.memset(q[:, :, :, :], 0.0).then_inc(q_zero, 1)
            dve.memset(qp_f[:, :, :], 0.0).then_inc(q_zero, 1)
            dve.memset(olat[:, :, NDEC:TOK - SEQ], 0.0).then_inc(olat_ok, 1)
            dve.wait_ge(q_in, 80)
            dve.tensor_copy(qc_f[:, :, :].rearrange("p a (s h) -> p a s h", s=NDEC),
                            q[:, :, :, :].rearrange("p a h s -> p a s h")).then_inc(qc_f_ok, 1)
            dve.wait_ge(qc_f_ok, 1)
            dve.wait_ge(q_zero, 2)
            dve.tensor_copy(qp_f[:, :, :].rearrange("p a (s c) -> p a s c", s=NDEC)[:, :, :, 0:NH],
                            qc_f[:, :, :].rearrange("p a (s h) -> p a s h", s=NDEC)).then_inc(qp_f_ok, 1)
            dve.wait_ge(qp_f_ok, 1)
            dve.wait_ge(q_hi, 2)
            split(dve, qp[:, 1, :, :], qp_f[:, :, :], qp[:, 0, :, :]).then_inc(q_ok, 1)
            split(dve, qc[:, 1, :, :], qc_f[:, :, :], qc[:, 0, :, :]).then_inc(q_ok, 1)
            for n in range(STEPS):
                dve.wait_ge(keys_hi, 2 * n + 1)
                split(dve, ckeys[n % 2][:, 1, :, :], ps_c[n % 2][:, :], ckeys[n % 2][:, 0, :, :])
                dve.wait_ge(keys_hi, 2 * n + 2)
                split(dve, rkeys[n % 2][:, 1, :, :], ps_r[n % 2][:, 0:2 * P], rkeys[n % 2][:, 0, :, :]).then_inc(keys_ok, 1)
            dve.wait_ge(new_in, 32)
            dve.wait_ge(new_ok, 1)
            dve.tensor_tensor_reduce(out=sc[:, PAST:PAST + NDEC], in0=ps_new[0:SH, 0:NDEC], in1=own[:, :], scale=1.0,
                                     scalar=3 * NEG, op0=ALU.add, op1=ALU.max, accum_out=top[:, 4:5])
            for c in range(4):
                dve.wait_ge(s_ok, STEPS - 3 + c)
                dve.tensor_scalar(sc[:, 512 * c:512 * c + 512], ps_s[c][0:SH, :], 1.0, None, ALU.mult, ALU.max,
                                  accum_out=top[:, c:c + 1]).then_inc(s_sb, 1)
            dve.wait_ge(s_sb, 4)
            dve.tensor_scalar(low[:, :], top[:, :], -SCALE, None, ALU.mult, ALU.min, accum_out=bias).then_inc(bias_ok, 1)
            dve.wait_ge(exp_ok, 1)
            dve.reciprocal(inverse, total).then_inc(inv_ok, 1)
            dve.wait_ge(inv_ok, 1)
            dve.tensor_scalar(sc[:, :], sc[:, :], inverse, None, ALU.mult).then_inc(p_ok, 1)
            dve.wait_ge(pt_turned, 2)
            dve.tensor_scalar(pt[:, RUN // 2:RUN, :], bank[1][:, :], 1.0, None, ALU.mult).then_inc(pt_ok, 1)

        @block.tensor
        def _(pe):
            def scores(n):
                s, c = n // 4, n % 4
                at = slice(s * SH, s * SH + SH)
                pe.wait_ge(keys_ok, n + 1)
                for k, (a, b) in enumerate(PARTS):
                    pe.matmul(ps_s[c][0:SH, :], qp[:, a, 0, at], ckeys[n % 2][:, b, :, :],
                              start=s == 0 and k == 0, stop=False)
                for half in range(2):
                    for k, (a, b) in enumerate(PARTS):
                        mm = pe.matmul(ps_s[c][0:SH, :].rearrange("q (t a k) -> q t a k", t=2, a=2)[:, :, half, :],
                                       qp[:, a, 1 + half, at], rkeys[n % 2][:, b, :, :], start=False,
                                       stop=s == NDEC - 1 and half == 1 and k == 2)
                mm.then_inc(s_ok, 1)

            for n in range(STEPS):
                s, c = n // 4, n % 4
                if c == 0:
                    pe.wait_ge(cache_in[s], 32)
                if n >= 2:
                    pe.wait_ge(keys_ok, n - 1)
                for j in range(4):
                    pe.transpose(ps_c[n % 2][:, j * P:j * P + P], cn[s][:, 4 * c + j, :], ident[:, :])
                for j in range(2):
                    at = 4 * c + 2 * j
                    mm = pe.transpose(ps_r[n % 2][:, j * P:j * P + P],
                                      rn[s][:, at:at + 2, :].rearrange("p t r -> p (t r)"), ident[:, :])
                mm.then_inc(turned, 1)
                if n == 1:
                    pe.wait_ge(q_ok, 2)
                if n >= 1:
                    scores(n - 1)
            scores(STEPS - 1)
            pe.wait_ge(keys_ok, STEPS)
            for k, (a, b) in enumerate(PARTS):
                pe.matmul(ps_new[0:SH, 0:NDEC], qc[:, a, 0, :], kt[:, NT - 1, 2 * b, 0:NDEC], start=k == 0, stop=False)
            for k, (a, b) in enumerate(PARTS):
                mm = pe.matmul(ps_new[0:SH, 0:NDEC], qc[:, a, 1, :], kt[:, NT - 1, 2 * b + 1, 0:NDEC],
                               start=False, stop=k == 2)
            mm.then_inc(new_ok, 1)
            pe.wait_ge(p_ok, 1)
            for part_ in range(2):
                for j in range(RUN // 2):
                    at = (part_ * RUN // 2 + j) * P
                    mm = pe.transpose(bank[part_][:, j * SH:j * SH + SH], sc[:, at:at + P], ident[0:SH, 0:SH])
                mm.then_inc(pt_turned, 1)
            pe.transpose(ps_new[0:NDEC, 0:SH], sc[:, PAST:PAST + NDEC], ident[0:SH, 0:SH]).then_inc(pt_turned, 1)
            pe.wait_ge(pt_ok, 3)
            pe.wait_ge(new_in, 32)
            for s in range(NDEC):
                at = slice(s * NH, s * NH + NH)
                out = ps_s[s // 4][0:NH, s % 4 * R:s % 4 * R + R]
                pe.matmul(out, ptn[:, at], cnew[:, :], start=True, stop=False)
                for j in range(RUN):
                    mm = pe.matmul(out, pt[:, j, at], cn[s][:, j, :], start=False, stop=j == RUN - 1)
                if s % 4 == 3:
                    mm.then_inc(o_ok, 1)
            pe.wait_ge(o_sb, 2)
            for s in range(NDEC):
                mm = pe.transpose(ps_o[:, s * NH:s * NH + NH], o[:, s, :], ident[0:NH, 0:NH])
            mm.then_inc(o_turned, 1)


def weight_order():
    order = [("U", g) for g in range(NG)] + [("ZP", g) for g in range(NG)] + [("ZA", h) for h in range(NH)]
    for pair in range(KD // 2):
        for n in (2 * pair, 2 * pair + 1):
            order += [("GA", n), ("GP", n), ("OA", n)]
        order.append(("OP", 2 * pair))
    return order + [("WO", n) for n in range(KD)]


ORDER = weight_order()
NW = len(ORDER)
AT = {tile: k for k, tile in enumerate(ORDER)}
POOLED = [2 * g + 2 for g in range(NG)]
POOLED_SPLIT = [k + 1 for k in POOLED]
POOL_MM = [k + 2 for k in POOLED]
POOL_GATE = [k + 1 for k in POOL_MM]
POOL_GATE_SPLIT = [k + 2 for k in POOL_MM]
LATENT_SPLIT = [AT["ZA", h] - 2 for h in range(NH)]
H_SPLIT = [AT["WO", 0] + n for n in range(4)]
SQUARES = [1, 2, 3, 3]
FINAL = [AT["GA", 0] + 1 + s for s in range(4)]
OP_STEPS = [AT["OP", n] for n in range(0, KD, 2)]
CARRY = AT["ZA", 6]


def merge(nc, io):
    with ExitStack() as ctx:
        def sb(name, shape, dt=f32):
            return ctx.enter_context(nc.sbuf_tensor("d_" + name, shape, dt))

        def sem(name):
            return ctx.enter_context(nc.semaphore("d_" + name))

        bank = [ctx.enter_context(nc.psum_tensor(f"d_ps{n}", [P, 512], f32)) for n in range(8)]
        ws = [sb(f"ws{n}", [P, KD, P]) for n in range(4)]
        wr = [sb(f"wr{n}", [P, 2, KD, P], f32r) for n in range(2)]
        hf = [sb(f"hf{n}", [P, 2, T]) for n in range(2)]
        ht = sb("ht", [P, 2, KD, T], f32r)
        gat = sb("gat", [P, 2, NH, T], f32r)
        gpl = sb("gpl", [P, 2, NG, T], f32r)
        mrg = sb("mrg", [P, 2, KD, T], f32r)
        u = sb("u", [P, NG, HIST + T])
        win = [sb(f"win{n}", [P, HIST + T]) for n in range(2)]
        pooled = sb("pooled", [P, T])
        pool2 = sb("pool2", [P, 2, T], f32r)
        olf = [sb(f"olf{n}", [P, T]) for n in range(2)]
        ols = [sb(f"ols{n}", [P, 2, T], f32r) for n in range(2)]
        sig = sb("sig", [P, T])
        zs = sb("zs", [P, NG, T])
        gated = sb("gated", [P, T])
        gated_pool = sb("gated_pool", [P, T])
        gate_p = [sb(f"gate_p{n}", [P, T]) for n in range(2)]
        ya = [sb(f"ya{n}", [P, T]) for n in range(2)]
        yt = ya
        y = sb("y", [SUB, 4, D])
        gfin = sb("gfin", [SUB, D])
        ident = sb("ident", [P, P])
        wuv = sb("wuv", [P, 2, NH, R], f32r)
        wpl = sb("wpl", [P, 2, NG, R], f32r)
        pscale = sb("pscale", [P, NG])
        head = sb("head", [P, NG, HIST])
        hsum = sb("hsum", [P, NG, NDEC])
        pick = sb("pick", [P, 2, NDEC])
        t1 = sb("t1", [P, NDEC])
        t2 = sb("t2", [P, NDEC])
        t3 = sb("t3", [P, NDEC])
        fstat = sb("fstat", [SUB, 4, 3])
        half = sb("half", [SUB, 1])
        wuv_f = zs[:, :, 0:2 * R]
        wpl_f = u[:, :, HIST:HIST + R]
        hist = u[:, :, HIST + R:HIST + R + NDEC * HIST]
        junk = zs[0:SUB, :, 0:D // NG]

        const_in = sem("const_in")
        CONSTS = 16 * 5
        small_in, small_hi, small_ok = sem("small_in"), sem("small_hi"), sem("small_ok")
        hsum_ok, gated_p, gp_hi, gp_lo = sem("hsum_ok"), sem("gated_p"), sem("gp_hi"), sem("gp_lo")
        w_in = [sem(f"w_in{n}") for n in range(4)]
        w_hi, w_ok, tile_ok = sem("w_hi"), sem("w_ok"), sem("tile_ok")
        h_in, h_hi, h_ok = [sem("h_in0"), sem("h_in1")], sem("h_hi"), sem("h_ok")
        u_sb, win_step, sum_ok, pl_f, pl_hi, pl_ok = (
            sem("u_sb"), sem("win_step"), sem("sum_ok"), sem("pl_f"), sem("pl_hi"), sem("pl_ok"))
        pick_in, carried, head_ok = sem("pick_in"), sem("carried"), sem("head_ok")
        pm_ok = sem("pm_ok")
        sig_ok, silu_ok, gated_ok, gated_hi, gated_lo = (
            sem("sig_ok"), sem("silu_ok"), sem("gated_ok"), sem("gated_hi"), sem("gated_lo"))
        ol_in = [sem("ol_in0"), sem("ol_in1")]
        ol_hi, ol_ok = sem("ol_hi"), sem("ol_ok")
        sa_ok, sp_ok, ya_ok, yp_ok, m_ok, m_hi, m_lo = (
            sem("sa_ok"), sem("sp_ok"), sem("ya_ok"), sem("yp_ok"), sem("m_ok"), sem("m_hi"), sem("m_lo"))
        yt_sb, xt_ok, y_add = sem("yt_sb"), sem("xt_ok"), sem("y_add")
        ss_ok, rinv_ok, fvar_ok, y_ok, y_out, x_in = (
            sem("ss_ok"), sem("rinv_ok"), sem("fvar_ok"), sem("y_ok"), sem("y_out"), sem("x_in"))
        tail_out, hist_out = sem("tail_out"), sem("hist_out")

        pair_bank = {"GA": (0, 3), "GP": (1, 4), "OA": (2, 5)}

        def out_bank(kind, n):
            if kind == "U":
                return 4 + n
            if kind == "ZP":
                return n
            if kind == "ZA":
                return 2 + n % 2
            if kind == "WO":
                return n % 2
            if kind == "OP":
                return 6
            return pair_bank[kind][n % 2]

        pm_bank = lambda g: 4 + g
        o_bank = lambda h: h % 2
        xt_bank = lambda n: 2 + n % 2
        levels = [w.bit_length() - 1 for w in WINDOWS]
        win_steps = sum(levels) + NG * 4

        block = ctx.enter_context(nc.Block())

        @block.sync
        def _(sp):
            def load_weights(k):
                sp.dma_start(ws[k % 4][:, :, :], io["w"][k % NW, :, :].rearrange("p (k c) -> p k c", k=KD)
                             ).then_inc(w_in[k % 4], 16)

            def load_h(c, quarter):
                sp.dma_start(hf[quarter % 2][:, :, :], io["ht"][:, 2 * quarter:2 * quarter + 2, bass.ds(c * T, T)]
                             ).then_inc(h_in[quarter % 2], 16)

            def load_latent(c, h):
                sp.dma_start(olf[h % 2][:, :], io["olat"][:, h, bass.ds(c * T, T)]).then_inc(ol_in[h % 2], 16)

            def load_pick(c):
                sp.dma_start(pick[:, :, :], io["pick"][bass.ds(c, 1), :, :, :].rearrange("a p b n -> (a p) b n")
                             ).then_inc(pick_in, 16)

            load_h(0, 0)
            load_h(0, 1)
            for k in range(4):
                load_weights(k)
            for quarter in (2, 3):
                sp.wait_ge(h_ok, quarter - 1)
                load_h(0, quarter)
            for slot in (0, 1):
                sp.wait_ge(h_ok, slot + 3)
                load_h(1, slot)
            sp.dma_start(ident[:, :], io["ident"]).then_inc(const_in, 16)
            sp.dma_start(pscale[:, :], io["pool_scale"]).then_inc(const_in, 16)
            sp.dma_start(head[:, :, :], io["head"]).then_inc(const_in, 16)
            sp.dma_start(hist, io["hist_t"]).then_inc(const_in, 16)
            sp.dma_start(gfin[:, :], io["g_final"].partition_broadcast(SUB)).then_inc(const_in, 16)
            load_pick(0)
            load_latent(0, 0)
            load_latent(0, 1)
            sp.dma_start(io["hist_out"], io["hist"][:, 1:HIST, :]).then_inc(hist_out, 16)
            with sp.Fori(0, NC) as c:
                follow = (c + 1) % NC
                for k in range(NW):
                    wait_all(sp, const_in, CONSTS, (w_ok, NW * c + k + 1))
                    load_weights(k + 4)
                    if k in H_SPLIT:
                        quarter = H_SPLIT.index(k)
                        wait_all(sp, const_in, CONSTS, (h_ok, 4 * c + quarter + 5))
                        load_h(follow if quarter < 2 else (c + 2) % NC, (quarter + 2) % 4)
                    if k == AT["ZA", 1]:
                        wait_all(sp, const_in, CONSTS, (sum_ok, NG * c + NG))
                        load_pick(follow)
                    if k == FINAL[3] + 1:
                        wait_all(sp, const_in, CONSTS, (y_ok, 4 * c + 4))
                        sp.dma_start(io["y"][bass.ds(c * T, T), :].rearrange("(s p) d -> p s d", p=SUB),
                                     y[:, :, :]).then_inc(y_out, 16)
                    if k == FINAL[3] + 5:
                        wait_all(sp, const_in, CONSTS, (y_out, 16 * c + 16))
                        sp.dma_start(y[:, :, :], io["x"][bass.ds(c * T, T), :].rearrange("(s p) d -> p s d", p=SUB)
                                     ).then_inc(x_in, 16)
                    if k - 1 in LATENT_SPLIT:
                        h = LATENT_SPLIT.index(k - 1)
                        wait_all(sp, const_in, CONSTS, (ol_ok, NH * c + h + 1))
                        load_latent(c if h + 2 < NH else follow, (h + 2) % NH)
            wait_all(sp, const_in, CONSTS, (y_ok, 4 * NC + 4))
            sp.dma_start(io["y"][NC * T:NC * T + T, :].rearrange("(s p) d -> p s d", p=SUB), y[:, :, :]).then_inc(y_out, 16)
            sp.dma_start(io["u_tail"], u[:, :, LAST:LAST + TAIL]).then_inc(tail_out, 16)
            sp.wait_ge(y_out, 16 * NC + 16)
            sp.wait_ge(x_in, 16 * NC)
            sp.wait_ge(tail_out, 16)
            sp.wait_ge(hist_out, 16)
            sp.wait_ge(pick_in, 16 * NC + 16)
            for n in range(2):
                sp.wait_ge(ol_in[n], 16 * (NH // 2 * NC + 1))
                sp.wait_ge(h_in[n], 16 * (2 * NC + 3))
            for n in range(4):
                sp.wait_ge(w_in[n], 16 * (NW // 4 * NC + 1))

        @block.scalar
        def _(act):
            act.dma_start(wuv_f, io["w_uv"]).then_inc(small_in, 16)
            act.dma_start(wpl_f, io["w_pool"]).then_inc(small_in, 16)

            def weights_high(c, k):
                act.wait_ge(w_in[k % 4], (c * (NW // 4) + k // 4 + 1) * 16)
                act.activation(wr[k % 2][:, 0, :, :], ws[k % 4][:, :, :], ACT.Copy).then_inc(w_hi, 1)

            def h_high(quarters, quarter):
                act.wait_ge(h_in[quarter % 2], quarters * 16 + 16)
                act.activation(ht[:, 0, 2 * quarter:2 * quarter + 2, :], hf[quarter % 2][:, :, :],
                               ACT.Copy).then_inc(h_hi, 1)

            h_high(0, 0)
            h_high(0, 1)
            weights_high(0, 0)
            weights_high(0, 1)
            h_high(1, 2)
            h_high(1, 3)
            act.wait_ge(small_in, 32)
            act.activation(wuv[:, 0, :, :].rearrange("p (g h) v -> p g (h v)", g=NG), wuv_f, ACT.Copy)
            act.activation(wpl[:, 0, :, :], wpl_f, ACT.Copy).then_inc(small_hi, 1)
            act.wait_ge(const_in, CONSTS)
            act.wait_ge(small_ok, 1)
            with act.Fori(0, NC) as c:
                for k, (kind, n) in enumerate(ORDER):
                    product = bank[out_bank(kind, n)][:, 0:T]
                    act.wait_ge(tile_ok, c * NW + k + 1)
                    if kind == "WO":
                        if n < 2:
                            act.wait_ge(m_lo, c * KD + KD)
                        else:
                            act.wait_ge(xt_ok, c * KD + n - 1)
                        act.activation(yt[n % 2][:, :], product, ACT.Copy).then_inc(yt_sb, 1)
                    weights_high(c, k + 2)
                    if k - 1 in [AT["ZA", h] for h in range(NH)]:
                        h = k - 1 - AT["ZA", 0]
                        act.wait_ge(gated_ok, c * NH + h + 1)
                        act.activation(gat[:, 0, h, :], gated[:, :], ACT.Copy).then_inc(gated_hi, 1)
                    if kind == "U":
                        act.activation(u[:, n, HIST:HIST + T], product, ACT.Copy).then_inc(u_sb, 1)
                    if kind in ("ZP", "ZA"):
                        z = n if kind == "ZP" else NG + n
                        if z >= 1:
                            act.wait_ge(silu_ok, c * (NG + NH) + z)
                        act.activation(sig[:, :], product, ACT.Sigmoid).then_inc(sig_ok, 1)
                    if kind == "GA":
                        if n >= 1:
                            act.wait_ge(ya_ok, c * KD + n)
                        act.activation(sig[:, :], product, ACT.Sigmoid).then_inc(sa_ok, 1)
                    if kind == "GP":
                        if n >= 2:
                            act.wait_ge(m_ok, c * KD + n - n % 2)
                        act.activation(gate_p[n % 2][:, :], product, ACT.Sigmoid).then_inc(sp_ok, 1)
                    if kind == "OP":
                        for a in range(2):
                            act.wait_ge(m_ok, c * KD + n + a + 1)
                            act.activation(mrg[:, 0, n + a, :], ya[a][:, :], ACT.Copy).then_inc(m_hi, 1)
                    if k in POOLED_SPLIT:
                        g = POOLED_SPLIT.index(k)
                        act.wait_ge(pl_f, c * NG + g + 1)
                        if g >= 1:
                            act.wait_ge(pm_ok, c * NG + g)
                        act.activation(pool2[:, 0, :], pooled[:, :], ACT.Copy).then_inc(pl_hi, 1)
                    if k in POOL_GATE_SPLIT:
                        g = POOL_GATE_SPLIT.index(k)
                        act.wait_ge(gated_p, c * NG + g + 1)
                        act.activation(gpl[:, 0, g, :], gated_pool[:, :], ACT.Copy).then_inc(gp_hi, 1)
                    if k in LATENT_SPLIT:
                        h = LATENT_SPLIT.index(k)
                        act.wait_ge(ol_in[h % 2], (c * (NH // 2) + h // 2 + 1) * 16)
                        act.activation(ols[h % 2][:, 0, :], olf[h % 2][:, :], ACT.Copy).then_inc(ol_hi, 1)
                    if k == CARRY:
                        act.wait_ge(pl_f, c * NG + NG)
                        act.activation(u[:, :, 0:HIST], u[:, :, T:HIST + T], ACT.Copy).then_inc(carried, 1)
                    if k in H_SPLIT:
                        quarter = H_SPLIT.index(k)
                        h_high(c * 2 + 2 + quarter // 2, quarter)
                    for s in range(4):
                        if SQUARES[s] == k:
                            act.wait_ge(w_ok, c * NW + 3)
                            if s >= 1:
                                act.wait_ge(ss_ok, c * 4 + s)
                            act.activation(junk, y[:, s, :].rearrange("p (g d) -> p g d", g=NG), ACT.Square,
                                           accum_out=fstat[:, s, 0:1]).then_inc(ss_ok, 1)
            act.wait_ge(y_add, KD * NC)
            for s in range(4):
                act.wait_ge(ss_ok, NC * 4 + s)
                act.activation(junk, y[:, s, :].rearrange("p (g d) -> p g d", g=NG), ACT.Square,
                               accum_out=fstat[:, s, 0:1]).then_inc(ss_ok, 1)

        @block.gpsimd
        def _(pool):
            pool.memset(half[:, :], -0.5).then_inc(win_step, 1)
            pool.wait_ge(const_in, CONSTS)
            pool.wait_ge(win_step, 1)

            def rms(count, s):
                wait_all(pool, const_in, CONSTS, (ss_ok, count + 1))
                pool.tensor_scalar(fstat[:, s, 1:2], fstat[:, s, 0:1], 1.0 / D, EPS, ALU.mult, ALU.add).then_inc(fvar_ok, 1)
                wait_all(pool, const_in, CONSTS, (fvar_ok, count + 1))
                pool.tensor_tensor(fstat[:, s, 2:3], fstat[:, s, 1:2], half[:, :], ALU.pow).then_inc(rinv_ok, 1)

            with pool.Fori(0, NC) as c:
                done = [0]

                def own(instruction):
                    done[0] += 1
                    instruction.then_inc(win_step, 1)
                    wait_all(pool, const_in, CONSTS, (win_step, c * win_steps + done[0] + 1))

                for g in range(NG):
                    wait_all(pool, const_in, CONSTS, (u_sb, c * NG + g + 1), *([(pl_f, c * NG + g)] if g else []))
                    source, start = u[:, g, :], 0
                    for level in range(levels[g]):
                        shift = 1 << level
                        start += shift
                        out = win[level % 2]
                        own(pool.tensor_tensor(out[:, start:HIST + T], source[:, start:HIST + T],
                                               source[:, start - shift:HIST + T - shift], ALU.add))
                        source = out
                    sums = source
                    own(pool.tensor_tensor(sums[:, HIST:2 * HIST], sums[:, HIST:2 * HIST], head[:, g, :], ALU.mult))
                    if g == 0:
                        wait_all(pool, const_in, CONSTS, (pick_in, c * 16 + 16))
                    d = slice(HIST + LAST, HIST + LAST + NDEC)
                    own(pool.tensor_tensor(t1[:, :], hsum[:, g, :], u[:, g, d], ALU.add))
                    own(pool.tensor_tensor(t2[:, :], t1[:, :], pick[:, 0, :], ALU.mult))
                    own(pool.tensor_tensor(t3[:, :], sums[:, d], pick[:, 1, :], ALU.mult))
                    pool.tensor_tensor(sums[:, d], t2[:, :], t3[:, :], ALU.add).then_inc(sum_ok, 1)
                    wait_all(pool, const_in, CONSTS, (sum_ok, c * NG + g + 1))
                    rms(c * 4 + g, g)
                assert done[0] == win_steps, (done[0], win_steps)
                pool.wait_ge(const_in, CONSTS)
                pool.memset(head[:, :, :], 1.0).then_inc(head_ok, 1)
            for s in range(4):
                rms(NC * 4 + s, s)

        @block.vector
        def _(dve):
            def weights_low(c, k):
                wait_all(dve, const_in, CONSTS, (w_hi, c * NW + k + 1))
                split(dve, wr[k % 2][:, 1, :, :], ws[k % 4][:, :, :], wr[k % 2][:, 0, :, :]).then_inc(w_ok, 1)

            def h_low(count, quarter):
                wait_all(dve, const_in, CONSTS, (h_hi, count))
                split(dve, ht[:, 1, 2 * quarter:2 * quarter + 2, :], hf[quarter % 2][:, :, :],
                      ht[:, 0, 2 * quarter:2 * quarter + 2, :]).then_inc(h_ok, 1)

            dve.memset(y[:, :, :], 0.0)
            for n in range(2):
                dve.wait_ge(h_hi, n + 1)
                split(dve, ht[:, 1, 2 * n:2 * n + 2, :], hf[n][:, :, :], ht[:, 0, 2 * n:2 * n + 2, :]).then_inc(h_ok, 1)
            for n in range(2):
                dve.wait_ge(w_hi, n + 1)
                split(dve, wr[n][:, 1, :, :], ws[n][:, :, :], wr[n][:, 0, :, :]).then_inc(w_ok, 1)
            for n in range(2, 4):
                dve.wait_ge(h_hi, n + 1)
                split(dve, ht[:, 1, 2 * n:2 * n + 2, :], hf[n % 2][:, :, :],
                      ht[:, 0, 2 * n:2 * n + 2, :]).then_inc(h_ok, 1)
            dve.wait_ge(small_hi, 1)
            split(dve, wuv[:, 1, :, :].rearrange("p (g h) v -> p g (h v)", g=NG), wuv_f,
                  wuv[:, 0, :, :].rearrange("p (g h) v -> p g (h v)", g=NG))
            split(dve, wpl[:, 1, :, :], wpl_f, wpl[:, 0, :, :])
            dve.wait_ge(const_in, CONSTS)
            for g, w in enumerate(WINDOWS):
                dve.tensor_reduce(hsum[:, g, :],
                                  hist[:, g, :].rearrange("p (n h) -> p n h", n=NDEC)[:, :, HIST - (w - 1):HIST],
                                  AX.X, ALU.add)
            dve.memset(u[:, :, 0:HIST], 0.0).then_inc(small_ok, 1)

            def zslot(kind, n):
                return n if kind == "ZP" else n % 3

            with dve.Fori(0, NC) as c:
                def add_output(n):
                    wait_all(dve, const_in, CONSTS, (xt_ok, c * KD + n + 1), (x_in, c * 16 + 16))
                    dve.tensor_tensor(y[:, :, n * P:n * P + P], y[:, :, n * P:n * P + P],
                                      bank[xt_bank(n)][0:SUB, :].rearrange("p (s d) -> p s d", s=4),
                                      ALU.add).then_inc(y_add, 1)

                for k, (kind, n) in enumerate(ORDER):
                    product = bank[out_bank(kind, n)][:, 0:T]
                    wait_all(dve, const_in, CONSTS, (tile_ok, c * NW + k + 1))
                    if kind != "OP":
                        weights_low(c, k + 2)
                    if k in POOL_GATE:
                        g = POOL_GATE.index(k)
                        wait_all(dve, const_in, CONSTS, (silu_ok, c * (NG + NH) + g + 1),
                                 *([(gp_lo, c * NG + g)] if g else []))
                        dve.scalar_tensor_tensor(gated_pool[:, :], bank[pm_bank(g)][:, 0:T], pscale[:, g:g + 1],
                                                 zs[:, g, :], ALU.mult, ALU.mult).then_inc(gated_p, 1)
                    if k - 1 in [AT["ZA", h] for h in range(NH)]:
                        h = k - 1 - AT["ZA", 0]
                        wait_all(dve, const_in, CONSTS, (gated_hi, c * NH + h + 1))
                        split(dve, gat[:, 1, h, :], gated[:, :], gat[:, 0, h, :]).then_inc(gated_lo, 1)
                    if kind in ("ZP", "ZA"):
                        z = n if kind == "ZP" else NG + n
                        wait_all(dve, const_in, CONSTS, (sig_ok, c * (NG + NH) + z + 1))
                        dve.tensor_tensor(zs[:, zslot(kind, n), :], product, sig[:, :], ALU.mult).then_inc(silu_ok, 1)
                    if kind == "ZA":
                        wait_all(dve, const_in, CONSTS, (silu_ok, c * (NG + NH) + z + 1),
                                 *([(gated_lo, c * NH + n)] if n else []))
                        dve.tensor_tensor(gated[:, :], bank[o_bank(n)][:, 0:T], zs[:, zslot(kind, n), :],
                                          ALU.mult).then_inc(gated_ok, 1)
                    if kind == "OA":
                        wait_all(dve, const_in, CONSTS, (sa_ok, c * KD + n + 1))
                        dve.tensor_tensor(ya[n % 2][:, :], product, sig[:, :], ALU.mult).then_inc(ya_ok, 1)
                    if kind == "OP":
                        wait_all(dve, const_in, CONSTS, (sp_ok, c * KD + n + 2))
                        for a in range(2):
                            dve.tensor_tensor(gate_p[a][:, :], bank[6 + a][:, 0:T], gate_p[a][:, :],
                                              ALU.mult).then_inc(yp_ok, 1)
                        for a in range(2):
                            wait_all(dve, const_in, CONSTS, (yp_ok, c * KD + n + a + 1), (ya_ok, c * KD + n + a + 1))
                            dve.tensor_tensor(ya[a][:, :], ya[a][:, :], gate_p[a][:, :], ALU.add).then_inc(m_ok, 1)
                        for a in range(2):
                            wait_all(dve, const_in, CONSTS, (m_hi, c * KD + n + a + 1), (m_ok, c * KD + n + a + 1))
                            split(dve, mrg[:, 1, n + a, :], ya[a][:, :], mrg[:, 0, n + a, :]).then_inc(m_lo, 1)
                        weights_low(c, k + 2)
                    if k in POOLED:
                        g = POOLED.index(k)
                        wait_all(dve, const_in, CONSTS, (sum_ok, c * NG + g + 1),
                                 *([(pl_ok, c * NG + g)] if g else []))
                        dve.scalar_tensor_tensor(pooled[:, :], win[(levels[g] - 1) % 2][:, HIST:HIST + T],
                                                 1.0 / WINDOWS[g], u[:, g, HIST:HIST + T], ALU.mult,
                                                 ALU.subtract).then_inc(pl_f, 1)
                    if k in POOLED_SPLIT:
                        g = POOLED_SPLIT.index(k)
                        wait_all(dve, const_in, CONSTS, (pl_hi, c * NG + g + 1))
                        split(dve, pool2[:, 1, :], pooled[:, :], pool2[:, 0, :]).then_inc(pl_ok, 1)
                    if k in POOL_GATE_SPLIT:
                        g = POOL_GATE_SPLIT.index(k)
                        wait_all(dve, const_in, CONSTS, (gp_hi, c * NG + g + 1))
                        split(dve, gpl[:, 1, g, :], gated_pool[:, :], gpl[:, 0, g, :]).then_inc(gp_lo, 1)
                    if k in LATENT_SPLIT:
                        h = LATENT_SPLIT.index(k)
                        wait_all(dve, const_in, CONSTS, (ol_hi, c * NH + h + 1))
                        split(dve, ols[h % 2][:, 1, :], olf[h % 2][:, :], ols[h % 2][:, 0, :]).then_inc(ol_ok, 1)
                    if k in H_SPLIT:
                        quarter = H_SPLIT.index(k)
                        h_low(c * 4 + 5 + quarter, quarter)
                    if k in FINAL:
                        s = FINAL.index(k)
                        wait_all(dve, const_in, CONSTS, (rinv_ok, c * 4 + s + 1))
                        dve.scalar_tensor_tensor(y[:, s, :], y[:, s, :], fstat[:, s, 2:3], gfin[:, :], ALU.mult,
                                                 ALU.mult).then_inc(y_ok, 1)
                    if kind == "WO" and n >= 2:
                        add_output(n - 2)
                add_output(KD - 2)
                add_output(KD - 1)
            for s in range(4):
                dve.wait_ge(rinv_ok, NC * 4 + s + 1)
                dve.scalar_tensor_tensor(y[:, s, :], y[:, s, :], fstat[:, s, 2:3], gfin[:, :], ALU.mult,
                                         ALU.mult).then_inc(y_ok, 1)

        @block.tensor
        def _(pe):
            pe.wait_ge(const_in, CONSTS)
            pe.wait_ge(small_ok, 1)

            def turn_output(c, n):
                pe.wait_ge(yt_sb, c * KD + n + 1)
                if n >= 2:
                    pe.wait_ge(y_add, c * KD + n - 1)
                for s in range(4):
                    mm = pe.transpose(bank[xt_bank(n)][0:SUB, s * P:s * P + P], yt[n % 2][:, s * SUB:s * SUB + SUB],
                                      ident[:, :])
                mm.then_inc(xt_ok, 1)

            with pe.Fori(0, NC) as c:
                for k, (kind, n) in enumerate(ORDER):
                    if kind == "ZA":
                        h = n
                        pe.wait_ge(ol_ok, c * NH + h + 1)
                        if h >= 2:
                            pe.wait_ge(gated_ok, c * NH + h - 1)
                        three_products(pe, bank[o_bank(h)][:, 0:T], lambda a, _: wuv[:, a, h, :],
                                       lambda b, _: ols[h % 2][:, b, :], 1)
                        pe.wait_ge(silu_ok, c * (NG + NH) + h + 3)
                    pe.wait_ge(w_ok, c * NW + k + 1)
                    if k == 0:
                        pe.wait_ge(h_ok, c * 4 + 4)
                    if kind in ("GA", "GP") and n == 0:
                        pe.wait_ge(gated_ok, c * NH + NH - (kind == "GA"))
                    if kind == "OA" and n == 0:
                        pe.wait_ge(gated_lo, c * NH + NH)
                    if kind == "OP" and n == 0:
                        pe.wait_ge(gp_lo, c * NG + NG)
                    if kind == "WO" and n >= 2:
                        pe.wait_ge(yt_sb, c * KD + n - 1)
                    w = wr[k % 2]
                    if kind == "OP":
                        for a in range(2):
                            mm = three_products(pe, bank[6 + a][:, 0:T], lambda part, j: w[:, part, NG * a + j, :],
                                                lambda part, j: gpl[:, part, j, :], NG)
                    else:
                        moving = {"OA": gat, "WO": mrg}.get(kind, ht)
                        done = 0
                        if kind == "WO" and n == 0:
                            done = KD - 2
                            three_products(pe, bank[out_bank(kind, n)][:, 0:T], lambda part, j: w[:, part, j, :],
                                           lambda part, j: moving[:, part, j, :], done, last=False)
                            pe.wait_ge(m_lo, c * KD + KD)
                        mm = three_products(pe, bank[out_bank(kind, n)][:, 0:T],
                                            lambda part, j: w[:, part, done + j, :],
                                            lambda part, j: moving[:, part, done + j, :], KD - done, first=done == 0)
                    mm.then_inc(tile_ok, 1)
                    if k in POOL_MM:
                        g = POOL_MM.index(k)
                        pe.wait_ge(pl_ok, c * NG + g + 1)
                        three_products(pe, bank[pm_bank(g)][:, 0:T], lambda a, _: wpl[:, a, g, :],
                                       lambda b, _: pool2[:, b, :], 1).then_inc(pm_ok, 1)
                    if kind == "WO" and n >= 1:
                        turn_output(c, n - 1)
                turn_output(c, KD - 1)


def finish(outs):
    y = outs["y"][T:]
    tail = outs["u_tail"].transpose(2, 1, 0).reshape(TAIL, NG * P)
    state = np.concatenate([outs["hist_out"], tail[HIST:, None, :]], axis=1)
    return (y[None, :SEQ], y[SEQ:SEQ + NDEC, None], outs["ckv"][None, None, :SEQ], outs["krope"][None, None, :SEQ],
            tail[None, None, :HIST], outs["ckv"][None, SEQ:SEQ + NDEC, None],
            outs["krope"][None, SEQ:SEQ + NDEC, None], state[None])


def build(nc, io):
    with ExitStack() as ctx:
        def sb(name, shape, dt=f32):
            return ctx.enter_context(nc.sbuf_tensor(name, shape, dt))

        keep = {
            "ident": sb("ident", [P, P]),
            "mask": sb("mask", [P, 512]),
            "kt": sb("kt", [P, NT, 4, P], f32r),
            "kv": sb("kv", [P, NT, 2, R], f32r),
        }
        project(nc, io, keep)
        attend(nc, io, keep)
        decode(nc, io, keep)
    merge(nc, io)


INPUTS = ("x", "w_lat", "w_uq_t", "w_uk_t", "w_uq_rope", "g_pre", "g_kv", "g_q", "cos", "sin", "mask", "ident",
          "w", "w_uv", "w_pool", "pool_scale", "head", "hist", "hist_t", "pick", "g_final",
          "pages", "page_part", "own", "cache_ckv", "cache_krope")
OUTPUTS = {"ckv": (ROWS, R), "krope": (ROWS, ROPE), "y": ((NC + 1) * T, D), "u_tail": (P, NG, TAIL),
           "hist_out": (NDEC, HIST - 1, NG * P)}
SCRATCH = {"olat": (P, NH, TOK), "ht": (P, KD, ROWS), "q": (NT, P, NH + NH // 2, P)}


def laid_out(x_prompt, x_sample, cache_ckv, cache_krope, state_pool, page_table, g_pre, w_in, g_q, w_uq,
             g_kv, w_uk, w_uv, w_o_att, w_pool, pool_scale, w_o_pool, w_out, g_final):
    c = np.ascontiguousarray
    w_in, w_uq, w_uk, w_uv = w_in[0], w_uq[0].reshape(QR, NH, NOPE + ROPE), w_uk[0], w_uv[0]
    x = np.zeros((ROWS, D), np.float32)
    x[:SEQ] = x_prompt[0]
    x[SEQ:SEQ + NDEC] = x_sample[:, 0]
    inv = (10000.0 ** (-np.arange(ROPE // 2) / (ROPE // 2))).astype(np.float32)
    pos = np.minimum(np.arange(ROWS), PAST).astype(np.float32)
    angle = np.tile(pos[:, None] * inv[None, :], (1, 2))
    by_tile = lambda a: c(a.reshape(NT, P, ROPE).transpose(1, 0, 2))
    mask = np.zeros((P, 512), np.float32)
    mask[:, 384:][np.arange(P)[None, :] > np.arange(P)[:, None]] = NEG
    rows = lambda a, k: c(a.reshape(k, P, -1).transpose(1, 0, 2))
    za = LAT
    up = za + NH * P
    zp = up + NG * P
    ga = zp + NG * P
    sources = {"ZA": w_in[:, za:up], "U": w_in[:, up:zp], "ZP": w_in[:, zp:ga], "GA": w_in[:, ga:ga + D],
               "GP": w_in[:, ga + D:], "OA": w_o_att[0], "WO": w_out[0]}
    w = np.empty((NW, P, KD, P), np.float32)
    for k, (kind, n) in enumerate(ORDER):
        if kind == "OP":
            for a in range(2):
                w[k, :, NG * a:NG * a + NG] = rows(w_o_pool[0][:, (n + a) * P:(n + a + 1) * P], NG)
        else:
            w[k] = rows(sources[kind][:, n * P:n * P + P], KD)
    count = np.minimum(np.array(WINDOWS)[:, None], np.arange(HIST)[None, :] + 1)
    head = np.broadcast_to((np.array(WINDOWS)[:, None] / count).astype(np.float32), (P, NG, HIST))
    own = np.full((NDEC, NH, NDEC), NEG, np.float32)
    own[np.arange(NDEC), :, np.arange(NDEC)] = 0
    own = own.reshape(NDEC * NH, NDEC)
    pick = np.zeros((NC, P, 2, NDEC), np.float32)
    pick[NC - 1, :, 0], pick[:NC - 1, :, 1] = 1, 1
    return {
        "x": x,
        "w_lat": rows(w_in[:, :LAT], KD),
        "w_uq_t": c(w_uq[:, :, :NOPE].transpose(2, 1, 0)),
        "w_uk_t": c(w_uk.transpose(2, 1, 0)),
        "w_uq_rope": rows(w_uq[:, :, NOPE:].reshape(QR, QROPE), KQ),
        "g_pre": c(g_pre[0]), "g_kv": c(g_kv[0]),
        "g_q": c(g_q[0].reshape(KQ, P).T),
        "cos": by_tile(np.cos(angle)), "sin": by_tile(np.sin(angle)),
        "mask": mask, "ident": np.eye(P, dtype=np.float32),
        "w": w.reshape(NW, P, KD * P),
        "w_uv": c(w_uv.reshape(R, NG, 2 * P)),
        "w_pool": c(w_pool[0].transpose(1, 0, 2)),
        "pool_scale": c(pool_scale[0].reshape(NG, P).T),
        "head": c(head), "pick": pick,
        "hist": c(state_pool[0]),
        "hist_t": c(state_pool[0].reshape(NDEC, HIST, NG, P).transpose(3, 2, 0, 1).reshape(P, NG, NDEC * HIST)),
        "g_final": c(g_final),
        "pages": c(np.repeat(page_table.T.astype(np.int32, copy=False), P // NPAGES, axis=0)),
        "page_part": c(np.broadcast_to((np.arange(P) % (P // NPAGES))[:, None], (P, NDEC)).astype(np.int32)),
        "own": own,
        "cache_ckv": c(cache_ckv[0].reshape(NPHYS * P // NPAGES, -1)),
        "cache_krope": c(cache_krope[0].reshape(NPHYS * P // NPAGES, -1)),
    }


def kernel(**inputs):
    import concourse.bacc as bacc
    from concourse.bass_utils import run_bass_kernel_spmd

    arrays = laid_out(**{name: np.asarray(array) for name, array in inputs.items()})
    nc = bacc.Bacc("TRN2", target_bir_lowering=False, num_devices=1)
    io = {name: nc.dram_tensor("in_" + name, arrays[name].shape, mybir.dt.from_np(arrays[name].dtype),
                               kind="ExternalInput").ap() for name in INPUTS}
    for shapes, kind in ((OUTPUTS, "ExternalOutput"), (SCRATCH, "Internal")):
        for name, shape in shapes.items():
            io[name] = nc.dram_tensor("out_" + name, shape, f32, kind=kind).ap()
    build(nc, io)
    if not nc.is_finalized():
        nc.finalize()
    result = run_bass_kernel_spmd(nc, [{"in_" + name: arrays[name] for name in INPUTS}], core_ids=[0]).results[0]
    return finish({name: result["out_" + name] for name in OUTPUTS})
```

```python
from contextlib import ExitStack

import numpy as np
import concourse.bass as bass
from concourse import mybir

f32 = mybir.dt.float32
f32r = mybir.dt.float32r
i32 = mybir.dt.int32
ALU = mybir.AluOpType
ACT = mybir.ActivationFunctionType
AX = mybir.AxisListType

P = 128
D = 1024
KD = D // P
SEQ = 2048
NDEC = 8
NH = 8
NOPE = 128
ROPE = 64
R = 128
QR = 256
KQ = QR // P
PAST = 2048
PAGE = 128
NPAGES = PAST // PAGE
NPHYS = NDEC * NPAGES + NDEC * NPAGES // 4
NG = 4
HIST = 15
WINDOWS = (2, 4, 8, 16)
EPS = 1e-6
SCALE = float((NOPE + ROPE) ** -0.5)
NEG = -1e30

PT = SEQ // P
NT = PT + 1
ROWS = NT * P
LAT = QR + R + ROPE
ABS = NH * R
QROPE = NH * ROPE
QCOLS = QROPE + ABS

NS, NTB, NPT = 3, 3, 4
PART = 8
SH = NDEC * NH
SROW = SH + NH
RUN = PAST // P
EARLY = 2
HG = 4
NGRP = NH // HG

T = 412
NC = -(-(SEQ + NDEC) // T)
TOK = NC * T
SUB = T // 4
TAIL = 23
LAST = SEQ - (NC - 1) * T


def split(e, low, source, high):
    return e.tensor_tensor(low, source, high.bitcast(f32), ALU.subtract)


def wait(e, sem, value):
    if not isinstance(value, int) or value > 0:
        e.wait_ge(sem, value)


def wait_all(e, known, count, *waits):
    held, counts = [], []
    for sem, value in waits:
        if not isinstance(value, int):
            register = e.alloc_register()
            e.reg_mov(register, value)
            held.append(register)
            value = register
        if not isinstance(value, int) or value > 0:
            counts.append((sem, value))
    e.wait_ge(known, count)
    for sem, value in counts:
        e.wait_ge(sem, value)
    for register in held:
        e.free_register(register)


def three_products(pe, out, stationary, moving, depth, first=True, last=True):
    for k in range(depth):
        for a, b in ((0, 0), (0, 1), (1, 0)):
            mm = pe.matmul(out, stationary(a, k), moving(b, k),
                           start=first and k == 0 and a + b == 0,
                           stop=last and k == depth - 1 and a == 1)
    return mm


def project(nc, io, keep):
    with ExitStack() as ctx:
        def sb(name, shape, dt=f32):
            return ctx.enter_context(nc.sbuf_tensor("a_" + name, shape, dt))

        def sem(name):
            return ctx.enter_context(nc.semaphore("a_" + name))

        ident, kt, kv = keep["ident"], keep["kt"], keep["kv"]
        ps = [ctx.enter_context(nc.psum_tensor(f"a_ps{n}", [P, 512], f32)) for n in range(8)]
        ps_x, ps_lat, ps_norm, ps_q = ps[0:2], ps[2], ps[3], ps[4:7]

        wlat = sb("wlat", [P, 2, KD, LAT], f32r)
        wq = sb("wq", [P, 2, KQ, QCOLS], f32r)
        gpre = sb("gpre", [P, D])
        gkv = sb("gkv", [P, R])
        gq = sb("gq", [P, KQ])
        cos = sb("cos", [P, NT, ROPE])
        sin = sb("sin", [P, NT, ROPE])
        half = sb("half", [P, 2])
        wlat_f = sb("wlat_f", [P, KD, LAT])
        wq_f = sb("wq_f", [P, KQ, QCOLS])
        wuq_t = sb("wuq_t", [P, NH, QR])
        wuk_t = sb("wuk_t", [P, NH, R])

        x = sb("x", [P, 2, D])
        junk = sb("junk", [P, D])
        h = sb("h", [P, D])
        hf = sb("hf", [P, KD, P])
        ht = sb("ht", [P, 2, KD, P], f32r)
        lat = sb("lat", [P, LAT])
        norm = sb("norm", [P, QR + R + 2 * ROPE])
        qt = sb("qt", [P, 2, KQ, P], f32r)
        qabs = sb("qabs", [P, ABS])
        qrot = sb("qrot", [P, NH, ROPE])
        qcos = sb("qcos", [P, NH, ROPE])
        qsin = sb("qsin", [P, NH, ROPE])
        kcos = sb("kcos", [P, ROPE])
        ksin = sb("ksin", [P, ROPE])
        qout = sb("qout", [P, NH + NH // 2, P])
        stat = sb("stat", [P, 12])
        x_ss, x_var, x_rinv = stat[:, 0:1], stat[:, 1:2], stat[:, 2:3]
        l_ss, l_var, l_rinv = stat[:, 4:6], stat[:, 6:8], stat[:, 8:10]
        C0 = QR
        K0 = QR + R
        H2 = ROPE // 2

        first_in, const_in, wlat_in, wq_in = sem("first_in"), sem("const_in"), sem("wlat_in"), sem("wq_in")
        FIRST, CONSTS = 16 * 2, 16 * 4
        half_ok, absorbed, wq_hi, weights_ok = (
            sem("half_ok"), sem("absorbed"), sem("wq_hi"), sem("weights_ok"))
        x_in, x_sq, x_rinv_ok, h_ok = sem("x_in"), sem("x_sq"), sem("x_rinv_ok"), sem("h_ok")
        xt_ok, hf_ok, h_out, ht_ok = sem("xt_ok"), sem("hf_ok"), sem("h_out"), sem("ht_ok")
        lat_ok, lat_sb, lat_sq, rinv_ok = sem("lat_ok"), sem("lat_sb"), sem("lat_sq"), sem("rinv_ok")
        ckv_ok, qn_ok, kr_ok, ckv_out, kr_out = (
            sem("ckv_ok"), sem("qn_ok"), sem("kr_ok"), sem("ckv_out"), sem("kr_out"))
        nt_ok, nt_hi, nt_lo = sem("nt_ok"), sem("nt_hi"), sem("nt_lo")
        q_ok, qabs_ok, qrot_ok = sem("q_ok"), sem("qabs_ok"), sem("qrot_ok")
        qt_ok, qout_a, qout_d, q_out = sem("qt_ok"), sem("qout_a"), sem("qout_d"), sem("q_out")
        dve_done, kv_hi = sem("dve_done"), sem("kv_hi")
        ht_hi, qcos_ok, ksq_ok, kro_ok = sem("ht_hi"), sem("qcos_ok"), sem("ksq_ok"), sem("kro_ok")
        var_ok = sem("var_ok")
        lvar_ok = sem("lvar_ok")

        def steps(e, step, columns=lambda: None, prepare=lambda: None):
            step(0, True, False, False, False)
            columns()
            step(1, True, True, False, False)
            prepare()
            step(2, True, True, True, False)
            with e.Fori(3, NT) as i:
                step(i, True, True, True, True)
            step(NT, False, True, True, True)
            step(NT + 1, False, False, True, True)
            step(NT + 2, False, False, False, True)

        block = ctx.enter_context(nc.Block())

        @block.sync
        def _(sp):
            sp.dma_start(x[:, 0, :], io["x"][0:P, :]).then_inc(x_in, 16)
            sp.dma_start(ident[:, :], io["ident"]).then_inc(first_in, 16)
            sp.dma_start(gpre[:, :], io["g_pre"].partition_broadcast(P)).then_inc(first_in, 16)
            sp.dma_start(wlat_f[:, :, :], io["w_lat"]).then_inc(wlat_in, 16)
            sp.dma_start(gkv[:, :], io["g_kv"].partition_broadcast(P)).then_inc(const_in, 16)
            sp.dma_start(gq[:, :], io["g_q"]).then_inc(const_in, 16)
            sp.dma_start(cos[:, :, :], io["cos"]).then_inc(const_in, 16)
            sp.dma_start(sin[:, :, :], io["sin"]).then_inc(const_in, 16)

            def step(i, pre, new, mid, old):
                if new:
                    n = i - 1
                    wait_all(sp, first_in, FIRST,
                             (hf_ok, 2 * n + 2))
                    sp.dma_start(io["ht"][:, :, bass.ds(n * P, P)], hf[:, :, :]).then_inc(h_out, 16)
                if old:
                    o = i - 3
                    wait_all(sp, first_in, FIRST,
                             (qout_a, 2 * o + 2),
                             (qout_d, o + 1))
                    sp.dma_start(io["q"][bass.ds(o, 1), :, :, :].rearrange("a p h t -> p (a h) t"),
                                 qout[:, :, :]).then_inc(q_out, 16)
                if new:
                    wait_all(sp, first_in, FIRST,
                             (ckv_ok, n + 1))
                    sp.dma_start(io["ckv"][bass.ds(n * P, P), :], norm[:, C0:K0]).then_inc(ckv_out, 16)
                    wait_all(sp, first_in, FIRST,
                             (kr_ok, n + 1))
                    sp.dma_start(io["krope"][bass.ds(n * P, P), :], norm[:, K0:K0 + ROPE]).then_inc(kr_out, 16)

            steps(sp, step)
            for s in (h_out, q_out, ckv_out, kr_out):
                sp.wait_ge(s, 16 * NT)
            sp.wait_ge(x_in, 16 * NT + 16)

        @block.gpsimd
        def _(pool):
            pool.memset(half[:, :], -0.5).then_inc(half_ok, 1)
            pool.wait_ge(half_ok, 1)
            pool.wait_ge(first_in, FIRST)

            def step(i, pre, new, mid, old):
                if pre:
                    wait_all(pool, first_in, FIRST,
                             (x_sq, i + 1),
                             (h_ok, i))
                    pool.tensor_scalar(x_var, x_ss, 1.0 / D, EPS, ALU.mult, ALU.add).then_inc(var_ok, 1)
                    wait(pool, var_ok, i + 1)
                    pool.tensor_tensor(x_rinv, x_var, half[:, 0:1], ALU.pow).then_inc(x_rinv_ok, 1)
                if new:
                    n = i - 1
                    wait_all(pool, const_in, CONSTS,
                             (lat_sq, 2 * n + 2),
                             (qn_ok, n),
                             (ckv_ok, n))
                    pool.tensor_scalar(l_var[:, 0:1], l_ss[:, 0:1], 1.0 / QR, EPS, ALU.mult, ALU.add)
                    pool.tensor_scalar(l_var[:, 1:2], l_ss[:, 1:2], 1.0 / R, EPS, ALU.mult, ALU.add).then_inc(lvar_ok, 1)
                    wait(pool, lvar_ok, n + 1)
                    pool.tensor_tensor(l_rinv, l_var, half[:, :], ALU.pow).then_inc(rinv_ok, 1)
                    tile_cos = cos[:, bass.ds(n, 1), :].rearrange("p a c -> p (a c)")
                    tile_sin = sin[:, bass.ds(n, 1), :].rearrange("p a c -> p (a c)")
                    wait(pool, kro_ok, n)
                    pool.tensor_tensor(kcos[:, :], lat[:, K0:K0 + ROPE], tile_cos, ALU.mult)
                    pool.tensor_tensor(ksin[:, :], lat[:, K0:K0 + ROPE], tile_sin, ALU.mult).then_inc(ksq_ok, 1)
                    wait(pool, ksq_ok, n + 1)
                    wait(pool, nt_ok, n)
                    wait(pool, kr_out, 16 * n)
                    pool.tensor_tensor(norm[:, K0:K0 + H2], kcos[:, 0:H2], ksin[:, H2:ROPE], ALU.subtract)
                    pool.tensor_tensor(norm[:, K0 + H2:K0 + ROPE], kcos[:, H2:ROPE], ksin[:, 0:H2],
                                       ALU.add).then_inc(kro_ok, 1)
                    wait_all(pool, const_in, CONSTS,
                             (kro_ok, n + 1))
                    pool.tensor_copy(norm[:, K0 + ROPE:K0 + 2 * ROPE], norm[:, K0:K0 + ROPE]).then_inc(kr_ok, 1)

            steps(pool, step)

        @block.scalar
        def _(act):
            act.wait_ge(first_in, FIRST)
            act.dma_start(wuq_t[:, :, :], io["w_uq_t"]).then_inc(wq_in, 16)
            act.dma_start(wuk_t[:, :, :], io["w_uk_t"]).then_inc(wq_in, 16)
            act.dma_start(wq_f[:, :, 0:QROPE], io["w_uq_rope"]).then_inc(wq_in, 16)

            def columns():
                act.wait_ge(wlat_in, 16)
                for half in range(2):
                    act.activation(wlat[:, 0, 4 * half:4 * half + 4, :], wlat_f[:, 4 * half:4 * half + 4, :],
                                   ACT.Copy).then_inc(wq_hi, 1)

            def step(i, pre, new, mid, old):
                if pre:
                    wait(act, x_in, 16 * i + 16)
                    wait(act, x_rinv_ok, i)
                    act.activation(junk[:, :], x[:, bass.ds(i % 2, 1), :].rearrange("p a d -> p (a d)"),
                                   ACT.Square, accum_out=x_ss).then_inc(x_sq, 1)
                    wait_all(act, first_in, FIRST, (h_ok, i))
                    following = (i + 1) % NT
                    act.dma_start(x[:, bass.ds((i + 1) % 2, 1), :], io["x"][bass.ds(following * P, P), :]).then_inc(x_in, 16)
                if mid:
                    m = i - 2
                    wait(act, nt_ok, m + 1)
                    act.activation(qt[:, 0, :, :], ps_norm[:, 0:QR], ACT.Copy).then_inc(nt_hi, 1)
                    act.activation(kt[:, bass.ds(m, 1), 0:2, :].rearrange("p a b t -> p (a b t)"),
                                   ps_norm[:, QR:512], ACT.Copy).then_inc(nt_hi, 1)
                if old:
                    o = i - 3
                    wait(act, q_out, 16 * o)
                    for a in range(2):
                        wait(act, qt_ok, 3 * o + 1 + a)
                        act.activation(qout[:, 4 * a:4 * a + 4, :], ps_q[a][:, :], ACT.Copy).then_inc(qout_a, 1)
                if new:
                    n = i - 1
                    wait(act, lat_ok, n + 1)
                    wait(act, ckv_ok, n)
                    wait(act, kro_ok, n)
                    act.activation(lat[:, :], ps_lat[:, 0:LAT], ACT.Copy).then_inc(lat_sb, 1)
                    wait(act, lat_sb, n + 1)
                    act.activation(junk[:, 0:QR], lat[:, 0:QR], ACT.Square, accum_out=l_ss[:, 0:1]).then_inc(lat_sq, 1)
                    act.activation(junk[:, QR:K0], lat[:, C0:K0], ACT.Square, accum_out=l_ss[:, 1:2]).then_inc(lat_sq, 1)
                if pre:
                    wait(act, h_out, 16 * i)
                    wait(act, ht_ok, i)
                    for a in range(2):
                        wait(act, xt_ok, 2 * i + 1 + a)
                        act.activation(hf[:, 4 * a:4 * a + 4, :], ps_x[a][:, :], ACT.Copy).then_inc(hf_ok, 1)
                if new:
                    wait(act, rinv_ok, n + 1)
                    wait(act, nt_ok, n)
                    act.activation(norm[:, 0:QR], lat[:, 0:QR], ACT.Copy, scale=l_rinv[:, 0:1]).then_inc(qn_ok, 1)
                if mid:
                    wait(act, qt_ok, 3 * m - 1)
                    for a in range(2):
                        wait(act, q_ok, 3 * m + 1 + a)
                        act.activation(qabs[:, 512 * a:512 * a + 512], ps_q[a][:, :], ACT.Copy).then_inc(qabs_ok, 1)

            steps(act, step, columns)

        @block.vector
        def _(dve):
            def columns():
                for half in range(2):
                    dve.wait_ge(wq_hi, half + 1)
                    at = slice(4 * half, 4 * half + 4)
                    low = split(dve, wlat[:, 1, at, :], wlat_f[:, at, :], wlat[:, 0, at, :])
                low.then_inc(weights_ok, 1)

            done = [1]

            def own(instruction):
                done[0] += 1
                instruction.then_inc(dve_done, 1)
                dve.wait_ge(dve_done, done[0])

            def prepare():
                dve.wait_ge(wq_in, 48)
                dve.wait_ge(const_in, CONSTS)
                for k in range(KQ):
                    own(dve.tensor_scalar(wq_f[:, k, 0:QROPE], wq_f[:, k, 0:QROPE], gq[:, k:k + 1], None, ALU.mult))
                    for a in range(2):
                        dve.wait_ge(absorbed, 2 * k + a + 1)
                        own(dve.tensor_scalar(wq_f[:, k, QROPE + 512 * a:QROPE + 512 * a + 512], ps[4 + 2 * a + k][:, :],
                                              gq[:, k:k + 1], None, ALU.mult))
                own(dve.tensor_copy(wq[:, 0, :, :], wq_f[:, :, :]))
                split(dve, wq[:, 1, :, :], wq_f[:, :, :], wq[:, 0, :, :]).then_inc(weights_ok, 1)

            def step(i, pre, new, mid, old):
                if mid:
                    m = i - 2
                    wait(dve, nt_hi, 2 * m + 2)
                    split(dve, qt[:, 1, :, :].rearrange("p k t -> p (k t)"), ps_norm[:, 0:QR],
                          qt[:, 0, :, :].rearrange("p k t -> p (k t)"))
                    split(dve, kt[:, bass.ds(m, 1), 2:4, :].rearrange("p a b t -> p (a b t)"), ps_norm[:, QR:512],
                          kt[:, bass.ds(m, 1), 0:2, :].rearrange("p a b t -> p (a b t)")).then_inc(nt_lo, 1)
                if pre:
                    wait(dve, x_rinv_ok, i + 1)
                    wait(dve, xt_ok, 2 * i)
                    dve.scalar_tensor_tensor(out=h[:, :], in0=x[:, bass.ds(i % 2, 1), :].rearrange("p a d -> p (a d)"),
                                             scalar=x_rinv, in1=gpre[:, :], op0=ALU.mult, op1=ALU.mult).then_inc(h_ok, 1)
                if old:
                    o = i - 3
                    wait(dve, qt_ok, 3 * o + 3)
                    wait(dve, q_out, 16 * o)
                    dve.tensor_copy(qout[:, NH:NH + NH // 2, :], ps_q[2][:, :]).then_inc(qout_d, 1)
                if pre:
                    wait(dve, hf_ok, 2 * i + 2)
                    wait(dve, lat_ok, i)
                    dve.tensor_copy(ht[:, 0, :, :], hf[:, :, :]).then_inc(ht_hi, 1)
                    wait(dve, ht_hi, i + 1)
                    split(dve, ht[:, 1, :, :], hf[:, :, :], ht[:, 0, :, :]).then_inc(ht_ok, 1)
                if new:
                    n = i - 1
                    wait(dve, rinv_ok, n + 1)
                    wait(dve, nt_ok, n)
                    wait(dve, ckv_out, 16 * n)
                    dve.scalar_tensor_tensor(out=norm[:, C0:K0], in0=lat[:, C0:K0], scalar=l_rinv[:, 1:2],
                                             in1=gkv[:, :], op0=ALU.mult, op1=ALU.mult).then_inc(ckv_ok, 1)
                    wait(dve, ckv_ok, n + 1)
                    high = kv[:, bass.ds(n, 1), 0, :].rearrange("p a r -> p (a r)")
                    dve.tensor_copy(high, norm[:, C0:K0]).then_inc(kv_hi, 1)
                    wait(dve, kv_hi, n + 1)
                    split(dve, kv[:, bass.ds(n, 1), 1, :].rearrange("p a r -> p (a r)"), norm[:, C0:K0],
                          high).then_inc(dve_done, 1)
                if mid:
                    tile_cos = cos[:, bass.ds(m, 1), :].to_broadcast([P, NH, ROPE])
                    tile_sin = sin[:, bass.ds(m, 1), :].to_broadcast([P, NH, ROPE])
                    wait(dve, q_ok, 3 * m + 3)
                    wait(dve, qt_ok, 3 * m)
                    q_rope = ps_q[2][:, :].rearrange("p (h c) -> p h c", h=NH)
                    dve.tensor_tensor(qcos[:, :, :], q_rope, tile_cos, ALU.mult)
                    dve.tensor_tensor(qsin[:, :, :], q_rope, tile_sin, ALU.mult).then_inc(qcos_ok, 1)
                    wait(dve, qcos_ok, m + 1)
                    dve.tensor_tensor(qrot[:, :, 0:H2], qcos[:, :, 0:H2], qsin[:, :, H2:ROPE], ALU.subtract)
                    dve.tensor_tensor(qrot[:, :, H2:ROPE], qcos[:, :, H2:ROPE], qsin[:, :, 0:H2], ALU.add).then_inc(qrot_ok, 1)

            steps(dve, step, columns, prepare)

        @block.tensor
        def _(pe):
            def prepare():
                pe.wait_ge(wq_in, 48)
                for k in range(KQ):
                    for a in range(2):
                        for hh in range(4):
                            head = 4 * a + hh
                            mm = pe.matmul(ps[4 + 2 * a + k][:, hh * R:hh * R + R], wuq_t[:, head, k * P:k * P + P],
                                           wuk_t[:, head, :], start=True, stop=True)
                        mm.then_inc(absorbed, 1)

            pe.wait_ge(first_in, FIRST)

            def step(i, pre, new, mid, old):
                if mid:
                    m = i - 2
                    wait(pe, qn_ok, m + 1)
                    wait(pe, ckv_ok, m + 1)
                    wait(pe, kr_ok, m + 1)
                    wait(pe, nt_lo, m)
                    for k in range(4):
                        mm = pe.transpose(ps_norm[:, k * P:k * P + P], norm[:, k * P:k * P + P], ident[:, :])
                    mm.then_inc(nt_ok, 1)
                if old:
                    o = i - 3
                    for a in range(2):
                        wait(pe, qabs_ok, 2 * o + 2)
                        for hh in range(4):
                            c = (4 * a + hh) * R
                            mm = pe.transpose(ps_q[a][:, hh * P:hh * P + P], qabs[:, c:c + R], ident[:, :])
                        mm.then_inc(qt_ok, 1)
                if new:
                    n = i - 1
                    if isinstance(n, int) and n == 0:
                        pe.wait_ge(weights_ok, 1)
                    wait(pe, ht_ok, n + 1)
                    wait(pe, lat_sb, n)
                    three_products(pe, ps_lat[:, 0:LAT], lambda a, k: ht[:, a, k, :],
                                   lambda b, k: wlat[:, b, k, :], KD).then_inc(lat_ok, 1)
                if old:
                    wait(pe, qrot_ok, o + 1)
                    for hh in range(NH // 2):
                        mm = pe.transpose(ps_q[2][:, hh * P:hh * P + P],
                                          qrot[:, 2 * hh:2 * hh + 2, :].rearrange("p h c -> p (h c)"), ident[:, :])
                    mm.then_inc(qt_ok, 1)
                if pre:
                    wait(pe, h_ok, i + 1)
                    wait(pe, hf_ok, 2 * i)
                    for k in range(KD):
                        mm = pe.transpose(ps_x[k // 4][:, k % 4 * P:k % 4 * P + P], h[:, k * P:k * P + P], ident[:, :])
                        if k % 4 == 3:
                            mm.then_inc(xt_ok, 1)
                if mid:
                    if isinstance(m, int) and m == 0:
                        pe.wait_ge(weights_ok, 2)
                    wait(pe, nt_lo, m + 1)
                    for group, columns in ((0, QROPE), (1, QROPE + 512), (2, 0)):
                        if group == 2:
                            wait(pe, qout_d, m)
                        else:
                            wait(pe, qout_a, 2 * m)
                        three_products(pe, ps_q[group][:, :], lambda a, k: qt[:, a, k, :],
                                       lambda b, k: wq[:, b, k, columns:columns + 512], KQ).then_inc(q_ok, 1)

            steps(pe, step, prepare=prepare)


def attend_orders():
    units = PT * NGRP
    tiles = lambda u: u // NGRP + 1
    chunks = lambda u: -(-tiles(u) // 4)
    parts = lambda u: -(-tiles(u) // PART)
    width = lambda u, n, size: min(size, tiles(u) - size * n)
    scores = [("S", u, h, c) for u in range(units) for h in range(HG) for c in range(chunks(u))]
    turns = [("T", u, j) for u in range(units) for j in range(tiles(u))]
    at_s = {step[1:]: n for n, step in enumerate(scores)}
    at_t = {step[1:]: n for n, step in enumerate(turns)}
    heads = [(u, h) for u in range(units) for h in range(HG)]
    queues = {
        "PE": [[("V", *t[1:]) for t in turns], list(turns), list(scores)],
        "ACT": [[("H", *t[1:]) for t in turns], [("E", u, h, p) for u, h in heads for p in range(parts(u))],
                [("O", u) for u in range(units)], [("Q", u) for u in range(units)]],
        "DVE": [[("L", *t[1:]) for t in turns], [("C", *s[1:]) for s in scores], [("B", u, h) for u, h in heads],
                [("I", u, h) for u, h in heads], [("P", u, h, p) for u, h in heads for p in range(parts(u))]],
    }

    def takes(step):
        kind, u = step[:2]
        if kind == "S":
            return 5 * max(0.107, 0.0535 * width(u, step[3], 4))
        if kind == "C":
            return 0.1 + 0.13 * width(u, step[3], 4)
        if kind == "E":
            return 0.25 + 0.106 * width(u, step[3], PART)
        if kind == "P":
            return 0.1 + 0.068 * width(u, step[3], PART)
        return {"T": 0.45, "V": 0.64, "H": 0.55, "L": 0.62, "O": 0.55, "Q": 1.1, "B": 0.2, "I": 0.35}[kind]

    def needs(step):
        kind, u, *at = step
        if kind == "S":
            n = at_s[step[1:]]
            out = [("Q", u)]
            if n >= NS:
                out.append(("C", *scores[n - NS][1:]))
            return out
        if kind == "C":
            out = [("S", u, *at)]
            if u >= 2:
                out.append(("T", u - 2, tiles(u - 2) - 1))
            return out
        if kind == "B":
            return [("C", u, at[0], chunks(u) - 1)]
        if kind == "E":
            return [("B", u, at[0])]
        if kind == "I":
            return [("E", u, at[0], parts(u) - 1)]
        if kind == "P":
            return [("I", u, at[0])]
        if kind == "Q":
            return [("S", u - 2, HG - 1, chunks(u - 2) - 1)] if u >= 2 else []
        if kind == "O":
            return [("V", u, tiles(u) - 1)]
        if kind == "V":
            out = [("L", u, *at)]
            if u >= 2 and at[0] == 0:
                out.append(("O", u - 2))
            return out
        n = at_t[step[1:]]
        if kind == "T":
            out = [("P", u, HG - 1, parts(u) - 1)]
            if n >= NTB:
                out.append(("L", *turns[n - NTB][1:]))
            return out
        if kind == "H":
            out = [("T", u, *at)]
            if n >= NPT:
                out.append(("V", *turns[n - NPT][1:]))
            return out
        return [("H", u, *at)]

    done, orders = {}, {e: [] for e in queues}
    now = {e: 0.0 for e in queues}
    while any(q for e in queues for q in queues[e]):
        engine = min((e for e in queues if any(queues[e])), key=lambda e: now[e])
        ready, later = None, []
        for queue in queues[engine]:
            if queue:
                times = [done.get(x) for x in needs(queue[0])]
                if None in times:
                    continue
                at = max(times, default=-1.0) + 0.1
                if at <= now[engine]:
                    ready = queue
                    break
                later.append(at)
        if ready is None:
            others = [now[e] for e in queues if e != engine and any(queues[e])]
            now[engine] = min(later + [max(now[engine], min(others, default=0.0)) + 0.05])
            continue
        step = ready.pop(0)
        now[engine] += takes(step)
        done[step] = now[engine]
        orders[engine].append(step)
    return orders


def attend(nc, io, keep, early):
    with ExitStack() as ctx:
        def sb(name, shape, dt=f32):
            return ctx.enter_context(nc.sbuf_tensor("b_" + name, shape, dt))

        def sem(name):
            return ctx.enter_context(nc.semaphore("b_" + name))

        ident, kt, kv, mask = keep["ident"], keep["kt"], keep["kv"], keep["mask"]
        ps = [ctx.enter_context(nc.psum_tensor(f"b_ps{n}", [P, 512], f32)) for n in range(8)]
        ps_s, ps_t, ps_o = ps[0:NS], ps[NS:NS + NTB], ps[6:8]
        qf = [sb(f"qf{n}", [P, 2, HG, P]) for n in range(2)]
        qs = [sb(f"qs{n}", [P, 3, HG, P], f32r) for n in range(2)]
        sp_ = [sb(f"p{n}", [P, SEQ]) for n in range(2 * HG)]
        pt = [sb(f"pt{n}", [P, 2, HG * P], f32r) for n in range(NPT)]
        ol = [sb(f"ol{n}", [P, HG * P]) for n in range(2)]
        top = sb("top", [P, 2 * HG, 4])
        low = sb("low", [P, 2 * HG, 4])
        bias = sb("bias", [P, 2 * HG])
        total = sb("total", [P, 2 * HG, 2])
        both = sb("both", [P, 2 * HG])
        inverse = sb("inverse", [P, 2 * HG])

        q_in = [sem("q_in0"), sem("q_in1")]
        q_hi, q_half, q_ok = sem("q_hi"), sem("q_half"), sem("q_ok")
        s_ok, s_sb, bias_ok, exp_ok, inv_ok, p_ok = (
            sem("s_ok"), sem("s_sb"), sem("bias_ok"), sem("exp_ok"), sem("inv_ok"), sem("p_ok"))
        sum_ok, mask_in = sem("sum_ok"), sem("mask_in")
        t_ok, pt_hi, pt_ok, v_ok, ol_ok = sem("t_ok"), sem("pt_hi"), sem("pt_ok"), sem("v_ok"), sem("ol_ok")
        o_out = [sem("o_out0"), sem("o_out1")]

        pages, run, rows, q, qc_f, qp_f, qc, qp = (
            early[name] for name in ("pages", "run", "rows", "q", "qc_f", "qp_f", "qc", "qp"))
        pages_in, rows_ok, dq_in, q_zero, qc_f_ok, qp_f_ok, dq_hi, dq_ok = (
            early[name] for name in ("pages_in", "rows_ok", "q_in", "q_zero", "qc_f_ok", "qp_f_ok", "q_hi", "q_ok"))

        orders = attend_orders()
        units = PT * NGRP
        number = {}
        for kind in "STVEP":
            for n, step in enumerate(x for order in orders.values() for x in order if x[0] == kind):
                number[step] = n
        parts = lambda u: -(-(u // NGRP + 1) // PART)
        tiles = lambda u: u // NGRP + 1
        chunks = lambda u: -(-tiles(u) // 4)
        last_turn = lambda u: number["T", u, tiles(u) - 1] + 1
        last_product = lambda u: number["V", u, tiles(u) - 1] + 1

        block = ctx.enter_context(nc.Block())

        @block.sync
        def _(sp):
            def load_q(u):
                i, g = u // NGRP, u % NGRP
                if u >= 2:
                    sp.wait_ge(q_hi, 2 * (u - 1))
                    sp.wait_ge(q_ok, u - 1)
                at = 2 * HG
                sp.dma_start(qf[u % 2][:, 0, :, :], io["q"][i, :, HG * g:HG * g + HG, :]).then_inc(q_in[u % 2], 16)
                for half in range(2):
                    pairs = io["q"][i, ROPE * half:ROPE * half + ROPE, at + 2 * g:at + 2 * g + 2, :]
                    for copy in range(2):
                        sp.dma_start(qf[u % 2][ROPE * copy:ROPE * copy + ROPE, 1, half:HG:2, :],
                                     pairs).then_inc(q_in[u % 2], 16)

            load_q(0)
            sp.dma_start(mask[:, :], io["mask"]).then_inc(mask_in, 16)
            load_q(1)
            sp.dma_start(pages[:, :], io["pages"]).then_inc(pages_in, 16)
            sp.dma_start(run[:, :], io["page_part"]).then_inc(pages_in, 16)
            sp.wait_ge(q_zero, 1)
            sp.dma_start(q[:, 0, :, :], io["q"][NT - 1, :, 0:NH, 0:NDEC]).then_inc(dq_in, 16)
            for half in range(2):
                for copy in range(2):
                    sp.dma_start(q[ROPE * copy:ROPE * copy + ROPE, 1 + copy, half:NH:2, :],
                                 io["q"][NT - 1, ROPE * half:ROPE * half + ROPE, NH:NH + NH // 2, 0:NDEC]
                                 ).then_inc(dq_in, 16)
            for u in range(2, units):
                load_q(u)
            for n in range(2):
                sp.wait_ge(o_out[n], 16 * units // 2)

        @block.gpsimd
        def _(pool):
            for u in range(units):
                pool.wait_ge(q_in[u % 2], 80 * (u // 2 + 1))
                pool.wait_ge(q_hi, 2 * (u + 1))
                if u >= 1:
                    pool.wait_ge(q_ok, u)
                split(pool, qs[u % 2][:, 1, :, :], qf[u % 2][:, 0, :, :], qs[u % 2][:, 0, :, :]).then_inc(q_half, 1)
                pool.wait_ge(q_half, u + 1)
                split(pool, qs[u % 2][ROPE:P, 2, :, :], qf[u % 2][ROPE:P, 1, :, :],
                      qs[u % 2][ROPE:P, 2, :, :]).then_inc(q_ok, 1)
            pool.wait_ge(q_ok, units)
            pool.wait_ge(rows_ok, 1)
            for sequence in range(EARLY):
                fetch_cache(pool, io, rows, sequence, early["cn"][sequence], early["rn"][sequence],
                            early["cache_in"][sequence])

        @block.scalar
        def _(act):
            for step in orders["ACT"]:
                kind, u = step[:2]
                if kind == "Q":
                    act.wait_ge(q_in[u % 2], 80 * (u // 2 + 1))
                    if u >= 2:
                        act.wait_ge(s_ok, number["S", u - 2, HG - 1, chunks(u - 2) - 1] + 1)
                    act.activation(qs[u % 2][:, 0, :, :], qf[u % 2][:, 0, :, :], ACT.Copy).then_inc(q_hi, 1)
                    act.activation(qs[u % 2][:, 2, :, :], qf[u % 2][:, 1, :, :], ACT.Copy).then_inc(q_hi, 1)
                elif kind == "E":
                    if step == ("E", 0, 0, 0):
                        act.wait_ge(qp_f_ok, 1)
                        act.activation(qp[:, 0, :, :], qp_f[:, :, :], ACT.Copy).then_inc(dq_hi, 1)
                        act.activation(qc[:, 0, :, :], qc_f[:, :, :], ACT.Copy).then_inc(dq_hi, 1)
                    _, _, h, part = step
                    row = (u % 2) * HG + h
                    keys = slice(part * PART * P, min(tiles(u), (part + 1) * PART) * P)
                    act.wait_ge(bias_ok, HG * u + h + 1)
                    act.activation(sp_[row][:, keys], sp_[row][:, keys], ACT.Exp, bias=bias[:, row:row + 1],
                                   scale=SCALE, accum_out=total[:, row, part:part + 1]).then_inc(exp_ok, 1)
                elif kind == "H":
                    n = number["T", u, step[2]]
                    act.wait_ge(t_ok, n + 1)
                    if n >= NPT:
                        act.wait_ge(v_ok, n - NPT + 1)
                    act.activation(pt[n % NPT][:, 0, :], ps_t[n % NTB][:, :], ACT.Copy).then_inc(pt_hi, 1)
                elif kind == "O":
                    i, g = u // NGRP, u % NGRP
                    act.wait_ge(v_ok, last_product(u))
                    if u >= 2:
                        act.wait_ge(o_out[u % 2], 16 * (u // 2))
                    act.activation(ol[u % 2][:, :], ps_o[u % 2][:, :], ACT.Copy).then_inc(ol_ok, 1)
                    act.wait_ge(ol_ok, u + 1)
                    act.dma_start(io["olat"][:, HG * g:HG * g + HG, i * P:i * P + P],
                                  ol[u % 2][:, :].rearrange("p (h t) -> p h t", h=HG)).then_inc(o_out[u % 2], 16)

        @block.vector
        def _(dve):
            dve.wait_ge(pages_in, 32)
            dve.scalar_tensor_tensor(rows[:, :], pages[:, :], PAGE // RUN, run[:, :], ALU.mult,
                                     ALU.add).then_inc(rows_ok, 1)
            dve.memset(q[:, :, :, :], 0.0).then_inc(q_zero, 1)
            dve.memset(qp_f[:, :, :], 0.0).then_inc(q_zero, 1)
            dve.wait_ge(dq_in, 80)
            dve.tensor_copy(qc_f[:, :, :].rearrange("p a (s h) -> p a s h", s=NDEC),
                            q[:, :, :, :].rearrange("p a h s -> p a s h")).then_inc(qc_f_ok, 1)
            dve.wait_ge(qc_f_ok, 1)
            dve.wait_ge(q_zero, 2)
            dve.tensor_copy(qp_f[:, :, :].rearrange("p a (s c) -> p a s c", s=NDEC)[:, :, :, 0:NH],
                            qc_f[:, :, :].rearrange("p a (s h) -> p a s h", s=NDEC)).then_inc(qp_f_ok, 1)
            dve.wait_ge(mask_in, 16)
            for step in orders["DVE"]:
                kind, u = step[:2]
                if kind == "C":
                    _, _, h, c = step
                    row = (u % 2) * HG + h
                    n = number["S", u, h, c]
                    keys = min(4, tiles(u) - 4 * c) * P
                    dve.wait_ge(s_ok, n + 1)
                    if u >= 2 and c == 0:
                        dve.wait_ge(t_ok, last_turn(u - 2))
                        dve.wait_ge(exp_ok, number["E", u - 2, h, parts(u - 2) - 1] + 1)
                    out, inp = sp_[row][:, 512 * c:512 * c + keys], ps_s[n % NS][:, 0:keys]
                    if c == chunks(u) - 1:
                        dve.tensor_tensor_reduce(out=out, in0=inp, in1=mask[:, 512 - keys:512], scale=1.0,
                                                 scalar=3 * NEG, op0=ALU.add, op1=ALU.max,
                                                 accum_out=top[:, row, c:c + 1]).then_inc(s_sb, 1)
                    else:
                        dve.tensor_scalar(out, inp, 1.0, None, ALU.mult, ALU.max,
                                          accum_out=top[:, row, c:c + 1]).then_inc(s_sb, 1)
                elif kind == "B":
                    h = step[2]
                    row = (u % 2) * HG + h
                    dve.wait_ge(s_sb, number["S", u, h, chunks(u) - 1] + 1)
                    dve.tensor_scalar(low[:, row, 0:chunks(u)], top[:, row, 0:chunks(u)], -SCALE, None, ALU.mult,
                                      ALU.min, accum_out=bias[:, row:row + 1]).then_inc(bias_ok, 1)
                elif kind == "I":
                    h = step[2]
                    row = (u % 2) * HG + h
                    dve.wait_ge(exp_ok, number["E", u, h, parts(u) - 1] + 1)
                    whole = total[:, row, 0:1]
                    if parts(u) == 2:
                        whole = both[:, row:row + 1]
                        dve.tensor_tensor(whole, total[:, row, 0:1], total[:, row, 1:2], ALU.add).then_inc(sum_ok, 1)
                        dve.wait_ge(sum_ok, HG * (u - PART * NGRP) + h + 1)
                    dve.reciprocal(inverse[:, row:row + 1], whole).then_inc(inv_ok, 1)
                elif kind == "P":
                    if step == ("P", 0, 0, 0):
                        dve.wait_ge(qp_f_ok, 1)
                        dve.wait_ge(dq_hi, 2)
                        split(dve, qp[:, 1, :, :], qp_f[:, :, :], qp[:, 0, :, :]).then_inc(dq_ok, 1)
                        split(dve, qc[:, 1, :, :], qc_f[:, :, :], qc[:, 0, :, :]).then_inc(dq_ok, 1)
                    _, _, h, part = step
                    row = (u % 2) * HG + h
                    keys = slice(part * PART * P, min(tiles(u), (part + 1) * PART) * P)
                    dve.wait_ge(inv_ok, HG * u + h + 1)
                    dve.tensor_scalar(sp_[row][:, keys], sp_[row][:, keys], inverse[:, row:row + 1], None,
                                      ALU.mult).then_inc(p_ok, 1)
                elif kind == "L":
                    n = number["T", u, step[2]]
                    dve.wait_ge(pt_hi, n + 1)
                    split(dve, pt[n % NPT][:, 1, :], ps_t[n % NTB][:, :], pt[n % NPT][:, 0, :]).then_inc(pt_ok, 1)

        @block.tensor
        def _(pe):
            for step in orders["PE"]:
                u = step[1]
                if step[0] == "S":
                    _, _, h, c = step
                    n = number[step]
                    first, keys = 4 * c, min(4, tiles(u) - 4 * c)
                    if h == 0 and c == 0:
                        pe.wait_ge(q_ok, u + 1)
                    if n >= NS:
                        pe.wait_ge(s_sb, n - NS + 1)
                    q = qs[u % 2]
                    pairs = ((0, 0), (0, 2), (1, 0), (2, 1), (2, 3))
                    for k, (a, b) in enumerate(pairs):
                        mm = pe.matmul(ps_s[n % NS][:, 0:keys * P], q[:, a, h, :], kt[:, first:first + keys, b, :],
                                       start=k == 0, stop=k == len(pairs) - 1)
                    mm.then_inc(s_ok, 1)
                elif step[0] == "T":
                    j, n = step[2], number[step]
                    if j == 0:
                        pe.wait_ge(p_ok, number["P", u, HG - 1, parts(u) - 1] + 1)
                    if n >= NTB:
                        pe.wait_ge(pt_ok, n - NTB + 1)
                    for h in range(HG):
                        mm = pe.transpose(ps_t[n % NTB][:, h * P:h * P + P],
                                          sp_[(u % 2) * HG + h][:, j * P:j * P + P], ident[:, :])
                    mm.then_inc(t_ok, 1)
                elif step[0] == "V":
                    j, n = step[2], number[step]
                    pe.wait_ge(pt_ok, n + 1)
                    if j == 0 and u >= 2:
                        pe.wait_ge(ol_ok, u - 1)
                    for k, (a, b) in enumerate(((0, 0), (0, 1), (1, 0))):
                        mm = pe.matmul(ps_o[u % 2][:, :], kv[:, j, a, :], pt[n % NPT][:, b, :],
                                       start=j == 0 and k == 0, stop=j == tiles(u) - 1 and k == 2)
                    mm.then_inc(v_ok, 1)


def early_decode(nc, ctx):
    def sb(name, shape, dt=f32):
        return ctx.enter_context(nc.sbuf_tensor("e_" + name, shape, dt))

    early = {name: ctx.enter_context(nc.semaphore("e_" + name))
             for name in ("pages_in", "rows_ok", "q_in", "q_zero", "qc_f_ok", "qp_f_ok", "q_hi", "q_ok")}
    early["cache_in"] = [ctx.enter_context(nc.semaphore(f"e_cache_in{s}")) for s in range(NDEC)]
    for name in ("pages", "run", "rows"):
        early[name] = sb(name, [P, NDEC], i32)
    early["cn"] = [sb(f"cn{s}", [P, RUN, R]) for s in range(EARLY)]
    early["rn"] = [sb(f"rn{s}", [P, RUN, ROPE]) for s in range(EARLY)]
    early["q"] = sb("q", [P, 3, NH, NDEC])
    early["qc_f"] = sb("qc_f", [P, 3, SH])
    early["qp_f"] = sb("qp_f", [P, 3, NDEC * SROW])
    early["qc"] = sb("qc", [P, 2, 3, SH], f32r)
    early["qp"] = sb("qp", [P, 2, 3, NDEC * SROW], f32r)
    return early


def fetch_cache(pool, io, rows, sequence, cn, rn, cache_in):
    at = bass.IndirectOffsetOnAxis(ap=rows[:, sequence:sequence + 1], axis=0)
    pool.indirect_dma_start(cn[:, :, :].rearrange("p t r -> p (t r)"), None, io["cache_ckv"], at).then_inc(cache_in, 16)
    pool.indirect_dma_start(rn[:, :, :].rearrange("p t r -> p (t r)"), None, io["cache_krope"],
                            at).then_inc(cache_in, 16)


def decode(nc, io, keep, early):
    with ExitStack() as ctx:
        def sb(name, shape, dt=f32):
            return ctx.enter_context(nc.sbuf_tensor("c_" + name, shape, dt))

        def sem(name):
            return ctx.enter_context(nc.semaphore("c_" + name))

        ident, kt = keep["ident"], keep["kt"]
        bank = [ctx.enter_context(nc.psum_tensor(f"c_ps{n}", [P, 512], f32)) for n in range(8)]
        ps_c, ps_r, ps_s, ps_new, ps_o = bank[0:2], bank[2:4], bank[4:8], bank[2], bank[3]
        PARTS = ((0, 0), (0, 1), (1, 0))
        STEPS = NDEC * 4
        rows, qc, qp, cache_in, q_ok = (early[name] for name in ("rows", "qc", "qp", "cache_in", "q_ok"))
        cn = early["cn"] + [sb(f"cn{s}", [P, RUN, R]) for s in range(EARLY, NDEC)]
        rn = early["rn"] + [sb(f"rn{s}", [P, RUN, ROPE]) for s in range(EARLY, NDEC)]
        cnew = sb("cnew", [NDEC, R])
        ckeys = [sb(f"ckeys{n}", [P, 2, 4, P], f32r) for n in range(2)]
        rkeys = [sb(f"rkeys{n}", [P, 2, 2, P], f32r) for n in range(2)]
        own = sb("own", [SH, NDEC])
        sc = sb("sc", [SH, PAST + NDEC])
        pt = sb("pt", [P, RUN, SH])
        ptn = sb("ptn", [NDEC, SH])
        o = sb("o", [NH, NDEC, R])
        top = sb("top", [SH, 5])
        low = sb("low", [SH, 5])
        stat = sb("stat", [SH, 3])
        bias, total, inverse = stat[:, 0:1], stat[:, 1:2], stat[:, 2:3]
        olat = sb("olat", [P, NH, TOK - SEQ])

        new_in = sem("new_in")
        turned, keys_hi, keys_ok, s_ok, new_ok = (
            sem("turned"), sem("keys_hi"), sem("keys_ok"), sem("s_ok"), sem("new_ok"))
        s_sb, bias_ok, exp_ok, inv_ok, p_ok = sem("s_sb"), sem("bias_ok"), sem("exp_ok"), sem("inv_ok"), sem("p_ok")
        o_sb, o_turned = sem("o_sb"), sem("o_turned")
        pt_turned, pt_ok, o_ok, olat_ok, olat_out = (
            sem("pt_turned"), sem("pt_ok"), sem("o_ok"), sem("olat_ok"), sem("olat_out"))

        block = ctx.enter_context(nc.Block())

        @block.sync
        def _(sp):
            sp.dma_start(own[:, :], io["own"]).then_inc(new_in, 16)
            sp.dma_start(cnew[:, :], io["ckv"][SEQ:SEQ + NDEC, :]).then_inc(new_in, 16)
            sp.wait_ge(olat_ok, 2)
            sp.dma_start(io["olat"][:, :, SEQ:TOK], olat[:, :, :]).then_inc(olat_out, 16)
            sp.wait_ge(olat_out, 16)

        @block.gpsimd
        def _(pool):
            for sequence in range(EARLY, NDEC):
                fetch_cache(pool, io, rows, sequence, cn[sequence], rn[sequence], cache_in[sequence])

        @block.scalar
        def _(act):
            for n in range(STEPS):
                act.wait_ge(turned, n + 1)
                if n >= 2:
                    act.wait_ge(s_ok, n - 1)
                act.activation(ckeys[n % 2][:, 0, :, :], ps_c[n % 2][:, :], ACT.Copy).then_inc(keys_hi, 1)
                act.activation(rkeys[n % 2][:, 0, :, :], ps_r[n % 2][:, 0:2 * P], ACT.Copy).then_inc(keys_hi, 1)
            act.wait_ge(bias_ok, 1)
            act.activation(sc[:, :], sc[:, :], ACT.Exp, bias=bias, scale=SCALE, accum_out=total).then_inc(exp_ok, 1)
            act.wait_ge(pt_turned, 1)
            act.activation(pt[:, 0:RUN // 2, :], bank[0][:, :], ACT.Copy).then_inc(pt_ok, 1)
            act.wait_ge(pt_turned, 3)
            act.activation(ptn[:, :], ps_new[0:NDEC, 0:SH], ACT.Copy).then_inc(pt_ok, 1)
            for n in range(2):
                act.wait_ge(o_ok, n + 1)
                act.activation(o[:, 4 * n:4 * n + 4, :], ps_s[n][0:NH, :], ACT.Copy).then_inc(o_sb, 1)
            act.wait_ge(o_turned, 1)
            act.activation(olat[:, :, 0:NDEC].rearrange("p h s -> p s h"),
                           ps_o[:, 0:SH].rearrange("p (s h) -> p s h", s=NDEC), ACT.Copy).then_inc(olat_ok, 1)

        @block.vector
        def _(dve):
            dve.memset(olat[:, :, NDEC:TOK - SEQ], 0.0).then_inc(olat_ok, 1)
            for n in range(STEPS):
                dve.wait_ge(keys_hi, 2 * n + 1)
                split(dve, ckeys[n % 2][:, 1, :, :], ps_c[n % 2][:, :], ckeys[n % 2][:, 0, :, :])
                dve.wait_ge(keys_hi, 2 * n + 2)
                split(dve, rkeys[n % 2][:, 1, :, :], ps_r[n % 2][:, 0:2 * P], rkeys[n % 2][:, 0, :, :]).then_inc(keys_ok, 1)
            dve.wait_ge(new_in, 32)
            dve.wait_ge(new_ok, 1)
            dve.tensor_tensor_reduce(out=sc[:, PAST:PAST + NDEC], in0=ps_new[0:SH, 0:NDEC], in1=own[:, :], scale=1.0,
                                     scalar=3 * NEG, op0=ALU.add, op1=ALU.max, accum_out=top[:, 4:5])
            for c in range(4):
                dve.wait_ge(s_ok, STEPS - 3 + c)
                dve.tensor_scalar(sc[:, 512 * c:512 * c + 512], ps_s[c][0:SH, :], 1.0, None, ALU.mult, ALU.max,
                                  accum_out=top[:, c:c + 1]).then_inc(s_sb, 1)
            dve.wait_ge(s_sb, 4)
            dve.tensor_scalar(low[:, :], top[:, :], -SCALE, None, ALU.mult, ALU.min, accum_out=bias).then_inc(bias_ok, 1)
            dve.wait_ge(exp_ok, 1)
            dve.reciprocal(inverse, total).then_inc(inv_ok, 1)
            dve.wait_ge(inv_ok, 1)
            dve.tensor_scalar(sc[:, :], sc[:, :], inverse, None, ALU.mult).then_inc(p_ok, 1)
            dve.wait_ge(pt_turned, 2)
            dve.tensor_scalar(pt[:, RUN // 2:RUN, :], bank[1][:, :], 1.0, None, ALU.mult).then_inc(pt_ok, 1)

        @block.tensor
        def _(pe):
            def scores(n):
                s, c = n // 4, n % 4
                at = slice(s * SH, s * SH + SH)
                pe.wait_ge(keys_ok, n + 1)
                for k, (a, b) in enumerate(PARTS):
                    pe.matmul(ps_s[c][0:SH, :], qp[:, a, 0, at], ckeys[n % 2][:, b, :, :],
                              start=s == 0 and k == 0, stop=False)
                for half in range(2):
                    for k, (a, b) in enumerate(PARTS):
                        mm = pe.matmul(ps_s[c][0:SH, :].rearrange("q (t a k) -> q t a k", t=2, a=2)[:, :, half, :],
                                       qp[:, a, 1 + half, at], rkeys[n % 2][:, b, :, :], start=False,
                                       stop=s == NDEC - 1 and half == 1 and k == 2)
                mm.then_inc(s_ok, 1)

            for n in range(STEPS):
                s, c = n // 4, n % 4
                if c == 0:
                    pe.wait_ge(cache_in[s], 32)
                if n >= 2:
                    pe.wait_ge(keys_ok, n - 1)
                for j in range(4):
                    pe.transpose(ps_c[n % 2][:, j * P:j * P + P], cn[s][:, 4 * c + j, :], ident[:, :])
                for j in range(2):
                    at = 4 * c + 2 * j
                    mm = pe.transpose(ps_r[n % 2][:, j * P:j * P + P],
                                      rn[s][:, at:at + 2, :].rearrange("p t r -> p (t r)"), ident[:, :])
                mm.then_inc(turned, 1)
                if n == 1:
                    pe.wait_ge(q_ok, 2)
                if n >= 1:
                    scores(n - 1)
            scores(STEPS - 1)
            pe.wait_ge(keys_ok, STEPS)
            for k, (a, b) in enumerate(PARTS):
                pe.matmul(ps_new[0:SH, 0:NDEC], qc[:, a, 0, :], kt[:, NT - 1, 2 * b, 0:NDEC], start=k == 0, stop=False)
            for k, (a, b) in enumerate(PARTS):
                mm = pe.matmul(ps_new[0:SH, 0:NDEC], qc[:, a, 1, :], kt[:, NT - 1, 2 * b + 1, 0:NDEC],
                               start=False, stop=k == 2)
            mm.then_inc(new_ok, 1)
            pe.wait_ge(p_ok, 1)
            for part_ in range(2):
                for j in range(RUN // 2):
                    at = (part_ * RUN // 2 + j) * P
                    mm = pe.transpose(bank[part_][:, j * SH:j * SH + SH], sc[:, at:at + P], ident[0:SH, 0:SH])
                mm.then_inc(pt_turned, 1)
            pe.transpose(ps_new[0:NDEC, 0:SH], sc[:, PAST:PAST + NDEC], ident[0:SH, 0:SH]).then_inc(pt_turned, 1)
            pe.wait_ge(pt_ok, 3)
            pe.wait_ge(new_in, 32)
            for s in range(NDEC):
                at = slice(s * NH, s * NH + NH)
                out = ps_s[s // 4][0:NH, s % 4 * R:s % 4 * R + R]
                pe.matmul(out, ptn[:, at], cnew[:, :], start=True, stop=False)
                for j in range(RUN):
                    mm = pe.matmul(out, pt[:, j, at], cn[s][:, j, :], start=False, stop=j == RUN - 1)
                if s % 4 == 3:
                    mm.then_inc(o_ok, 1)
            pe.wait_ge(o_sb, 2)
            for s in range(NDEC):
                mm = pe.transpose(ps_o[:, s * NH:s * NH + NH], o[:, s, :], ident[0:NH, 0:NH])
            mm.then_inc(o_turned, 1)


def weight_order():
    order = [("U", g) for g in range(NG)] + [("ZP", g) for g in range(NG)] + [("ZA", h) for h in range(NH)]
    for pair in range(KD // 2):
        for n in (2 * pair, 2 * pair + 1):
            order += [("GA", n), ("GP", n), ("OA", n)]
        order.append(("OP", 2 * pair))
    return order + [("WO", n) for n in range(KD)]


ORDER = weight_order()
NW = len(ORDER)
AT = {tile: k for k, tile in enumerate(ORDER)}
POOLED = [2 * g + 2 for g in range(NG)]
POOLED_SPLIT = [k + 1 for k in POOLED]
POOL_MM = [k + 2 + (k == POOLED[-1]) for k in POOLED]
POOL_GATE = [k + 1 for k in POOL_MM]
POOL_GATE_SPLIT = [k + 2 for k in POOL_MM]
LATENT_SPLIT = [AT["ZA", h] - 2 for h in range(NH)]
H_SPLIT = [AT["WO", 0] + n for n in range(4)]
SQUARES = [1, 2, 3, 3]
FINAL = [AT["GA", 0] + 1 + s for s in range(4)]
OP_STEPS = [AT["OP", n] for n in range(0, KD, 2)]
CARRY = AT["ZA", 6]


def merge(nc, io):
    with ExitStack() as ctx:
        def sb(name, shape, dt=f32):
            return ctx.enter_context(nc.sbuf_tensor("d_" + name, shape, dt))

        def sem(name):
            return ctx.enter_context(nc.semaphore("d_" + name))

        bank = [ctx.enter_context(nc.psum_tensor(f"d_ps{n}", [P, 512], f32)) for n in range(8)]
        ws = [sb(f"ws{n}", [P, KD, P]) for n in range(4)]
        wr = [sb(f"wr{n}", [P, 2, KD, P], f32r) for n in range(2)]
        hf = [sb(f"hf{n}", [P, 2, T]) for n in range(2)]
        ht = sb("ht", [P, 2, KD, T], f32r)
        gat = sb("gat", [P, 2, NH, T], f32r)
        gpl = sb("gpl", [P, 2, NG, T], f32r)
        mrg = sb("mrg", [P, 2, KD, T], f32r)
        u = sb("u", [P, NG, HIST + T])
        win = [sb(f"win{n}", [P, HIST + T]) for n in range(4)]
        pooled = sb("pooled", [P, T])
        pool2 = sb("pool2", [P, 2, T], f32r)
        olf = [sb(f"olf{n}", [P, T]) for n in range(2)]
        ols = [sb(f"ols{n}", [P, 2, T], f32r) for n in range(2)]
        sig = sb("sig", [P, T])
        zs = sb("zs", [P, NG, T])
        gated = sb("gated", [P, T])
        gated_pool = sb("gated_pool", [P, T])
        gate_p = [sb(f"gate_p{n}", [P, T]) for n in range(2)]
        ya = [sb(f"ya{n}", [P, T]) for n in range(2)]
        yt = ya
        y = sb("y", [SUB, 4, D])
        gfin = sb("gfin", [SUB, D])
        ident = sb("ident", [P, P])
        wuv = sb("wuv", [P, 2, NH, R], f32r)
        wpl = sb("wpl", [P, 2, NG, R], f32r)
        pscale = sb("pscale", [P, NG])
        head = sb("head", [P, NG, HIST])
        hsum = sb("hsum", [P, NG, NDEC])
        pick = sb("pick", [P, 2, NDEC])
        t1 = sb("t1", [P, NDEC])
        t2 = sb("t2", [P, NDEC])
        t3 = sb("t3", [P, NDEC])
        fstat = sb("fstat", [SUB, 4, 3])
        half = sb("half", [SUB, 1])
        wuv_f = zs[:, :, 0:2 * R]
        wpl_f = u[:, :, HIST:HIST + R]
        hist = u[:, :, HIST + R:HIST + R + NDEC * HIST]
        junk = zs[0:SUB, :, 0:D // NG]

        const_in = sem("const_in")
        CONSTS = 16 * 5
        small_in, small_hi, small_ok = sem("small_in"), sem("small_hi"), sem("small_ok")
        gated_p, gp_hi, gp_lo = sem("gated_p"), sem("gp_hi"), sem("gp_lo")
        w_in = [sem(f"w_in{n}") for n in range(4)]
        w_hi, w_ok, tile_ok = sem("w_hi"), sem("w_ok"), sem("tile_ok")
        h_in, h_hi, h_ok = [sem("h_in0"), sem("h_in1")], sem("h_hi"), sem("h_ok")
        u_sb, win_step, sum_ok, pl_f, pl_hi, pl_ok = (
            sem("u_sb"), sem("win_step"), sem("sum_ok"), sem("pl_f"), sem("pl_hi"), sem("pl_ok"))
        pick_in, carried, head_ok = sem("pick_in"), sem("carried"), sem("head_ok")
        pm_ok = sem("pm_ok")
        sig_ok, silu_ok, gated_ok, gated_hi, gated_lo = (
            sem("sig_ok"), sem("silu_ok"), sem("gated_ok"), sem("gated_hi"), sem("gated_lo"))
        ol_in = [sem("ol_in0"), sem("ol_in1")]
        ol_hi, ol_ok = sem("ol_hi"), sem("ol_ok")
        sa_ok, sp_ok, ya_ok, yp_ok, m_ok, m_hi, m_lo = (
            sem("sa_ok"), sem("sp_ok"), sem("ya_ok"), sem("yp_ok"), sem("m_ok"), sem("m_hi"), sem("m_lo"))
        yt_sb, xt_ok, y_add = sem("yt_sb"), sem("xt_ok"), sem("y_add")
        ss_ok, rinv_ok, fvar_ok, y_ok, y_out, x_in = (
            sem("ss_ok"), sem("rinv_ok"), sem("fvar_ok"), sem("y_ok"), sem("y_out"), sem("x_in"))
        tail_out, hist_out, y_zero = sem("tail_out"), sem("hist_out"), sem("y_zero")

        pair_bank = {"GA": (0, 3), "GP": (1, 4), "OA": (2, 5)}

        def out_bank(kind, n):
            if kind == "U":
                return 4 + n
            if kind == "ZP":
                return n
            if kind == "ZA":
                return 2 + n % 2
            if kind == "WO":
                return n % 2
            if kind == "OP":
                return 6
            return pair_bank[kind][n % 2]

        pm_bank = lambda g: 4 + g
        o_bank = lambda h: h % 2
        xt_bank = lambda n: 2 + n % 2
        levels = [w.bit_length() - 1 for w in WINDOWS]
        win_steps = sum(levels) + NG * 4

        block = ctx.enter_context(nc.Block())

        @block.sync
        def _(sp):
            def load_weights(k):
                sp.dma_start(ws[k % 4][:, :, :], io["w"][k % NW, :, :].rearrange("p (k c) -> p k c", k=KD)
                             ).then_inc(w_in[k % 4], 16)

            def load_h(c, quarter):
                sp.dma_start(hf[quarter % 2][:, :, :], io["ht"][:, 2 * quarter:2 * quarter + 2, bass.ds(c * T, T)]
                             ).then_inc(h_in[quarter % 2], 16)

            def load_latent(c, h):
                sp.dma_start(olf[h % 2][:, :], io["olat"][:, h, bass.ds(c * T, T)]).then_inc(ol_in[h % 2], 16)

            def load_pick(c):
                sp.dma_start(pick[:, :, :], io["pick"][bass.ds(c, 1), :, :, :].rearrange("a p b n -> (a p) b n")
                             ).then_inc(pick_in, 16)

            load_h(0, 0)
            load_h(0, 1)
            load_weights(0)
            load_weights(1)
            for quarter in (2, 3):
                sp.wait_ge(h_ok, quarter - 1)
                load_h(0, quarter)
            load_weights(2)
            load_weights(3)
            for slot in (0, 1):
                sp.wait_ge(h_ok, slot + 3)
                load_h(1, slot)
            sp.dma_start(ident[:, :], io["ident"]).then_inc(const_in, 16)
            sp.dma_start(pscale[:, :], io["pool_scale"]).then_inc(const_in, 16)
            sp.dma_start(head[:, :, :], io["head"]).then_inc(const_in, 16)
            sp.dma_start(hist, io["hist_t"]).then_inc(const_in, 16)
            sp.dma_start(gfin[:, :], io["g_final"].partition_broadcast(SUB)).then_inc(const_in, 16)
            load_pick(0)
            load_latent(0, 0)
            load_latent(0, 1)
            sp.dma_start(io["hist_out"], io["hist"][:, 1:HIST, :]).then_inc(hist_out, 16)
            with sp.Fori(0, NC) as c:
                follow = (c + 1) % NC
                for k in range(NW):
                    wait_all(sp, const_in, CONSTS, (w_ok, NW * c + k + 1))
                    load_weights(k + 4)
                    if k in H_SPLIT:
                        quarter = H_SPLIT.index(k)
                        wait_all(sp, const_in, CONSTS, (h_ok, 4 * c + quarter + 5))
                        load_h(follow if quarter < 2 else (c + 2) % NC, (quarter + 2) % 4)
                    if k == AT["ZA", 1]:
                        wait_all(sp, const_in, CONSTS, (sum_ok, NG * c + NG))
                        load_pick(follow)
                    if k == FINAL[3] + 1:
                        wait_all(sp, const_in, CONSTS, (y_ok, 4 * c + 4))
                        sp.dma_start(io["y"][bass.ds(c * T, T), :].rearrange("(s p) d -> p s d", p=SUB),
                                     y[:, :, :]).then_inc(y_out, 16)
                    if k == FINAL[3] + 5:
                        wait_all(sp, const_in, CONSTS, (y_out, 16 * c + 16))
                        sp.dma_start(y[:, :, :], io["x"][bass.ds(c * T, T), :].rearrange("(s p) d -> p s d", p=SUB)
                                     ).then_inc(x_in, 16)
                    if k - 1 in LATENT_SPLIT:
                        h = LATENT_SPLIT.index(k - 1)
                        wait_all(sp, const_in, CONSTS, (ol_ok, NH * c + h + 1))
                        load_latent(c if h + 2 < NH else follow, (h + 2) % NH)
            wait_all(sp, const_in, CONSTS, (y_ok, 4 * NC + 4))
            sp.dma_start(io["y"][NC * T:NC * T + T, :].rearrange("(s p) d -> p s d", p=SUB), y[:, :, :]).then_inc(y_out, 16)
            sp.dma_start(io["u_tail"], u[:, :, LAST:LAST + TAIL]).then_inc(tail_out, 16)
            sp.wait_ge(y_out, 16 * NC + 16)
            sp.wait_ge(x_in, 16 * NC)
            sp.wait_ge(tail_out, 16)
            sp.wait_ge(hist_out, 16)
            sp.wait_ge(pick_in, 16 * NC + 16)
            for n in range(2):
                sp.wait_ge(ol_in[n], 16 * (NH // 2 * NC + 1))
                sp.wait_ge(h_in[n], 16 * (2 * NC + 3))
            for n in range(4):
                sp.wait_ge(w_in[n], 16 * (NW // 4 * NC + 1))

        @block.scalar
        def _(act):
            def weights_high(c, k):
                act.wait_ge(w_in[k % 4], (c * (NW // 4) + k // 4 + 1) * 16)
                act.activation(wr[k % 2][:, 0, :, :], ws[k % 4][:, :, :], ACT.Copy).then_inc(w_hi, 1)

            def h_high(quarters, quarter):
                act.wait_ge(h_in[quarter % 2], quarters * 16 + 16)
                act.activation(ht[:, 0, 2 * quarter:2 * quarter + 2, :], hf[quarter % 2][:, :, :],
                               ACT.Copy).then_inc(h_hi, 1)

            h_high(0, 0)
            h_high(0, 1)
            act.dma_start(wpl_f, io["w_pool"]).then_inc(small_in, 16)
            act.dma_start(wuv_f, io["w_uv"]).then_inc(small_in, 16)
            weights_high(0, 0)
            weights_high(0, 1)
            h_high(1, 2)
            h_high(1, 3)
            act.wait_ge(small_in, 32)
            act.activation(wuv[:, 0, :, :].rearrange("p (g h) v -> p g (h v)", g=NG), wuv_f, ACT.Copy)
            act.activation(wpl[:, 0, :, :], wpl_f, ACT.Copy).then_inc(small_hi, 1)
            act.wait_ge(const_in, CONSTS)
            act.wait_ge(y_zero, 1)
            act.wait_ge(small_ok, 1)
            with act.Fori(0, NC) as c:
                for k, (kind, n) in enumerate(ORDER):
                    product = bank[out_bank(kind, n)][:, 0:T]
                    act.wait_ge(tile_ok, c * NW + k + 1)
                    if kind == "WO":
                        if n < 2:
                            act.wait_ge(m_lo, c * KD + KD)
                        else:
                            act.wait_ge(xt_ok, c * KD + n - 1)
                        act.activation(yt[n % 2][:, :], product, ACT.Copy).then_inc(yt_sb, 1)
                    weights_high(c, k + 2)
                    if k in LATENT_SPLIT:
                        h = LATENT_SPLIT.index(k)
                        act.wait_ge(ol_in[h % 2], (c * (NH // 2) + h // 2 + 1) * 16)
                        act.activation(ols[h % 2][:, 0, :], olf[h % 2][:, :], ACT.Copy).then_inc(ol_hi, 1)
                    if k - 1 in [AT["ZA", h] for h in range(NH)]:
                        h = k - 1 - AT["ZA", 0]
                        act.wait_ge(gated_ok, c * NH + h + 1)
                        act.activation(gat[:, 0, h, :], gated[:, :], ACT.Copy).then_inc(gated_hi, 1)
                    if kind == "U":
                        act.activation(u[:, n, HIST:HIST + T], product, ACT.Copy).then_inc(u_sb, 1)
                    if kind in ("ZP", "ZA"):
                        z = n if kind == "ZP" else NG + n
                        if z >= 1:
                            act.wait_ge(silu_ok, c * (NG + NH) + z)
                        act.activation(sig[:, :], product, ACT.Sigmoid).then_inc(sig_ok, 1)
                    if kind == "GA":
                        if n >= 1:
                            act.wait_ge(ya_ok, c * KD + n)
                        act.activation(sig[:, :], product, ACT.Sigmoid).then_inc(sa_ok, 1)
                    if kind == "GP":
                        if n >= 2:
                            act.wait_ge(m_ok, c * KD + n - n % 2)
                        act.activation(gate_p[n % 2][:, :], product, ACT.Sigmoid).then_inc(sp_ok, 1)
                    if kind == "OP":
                        for a in range(2):
                            act.wait_ge(m_ok, c * KD + n + a + 1)
                            act.activation(mrg[:, 0, n + a, :], ya[a][:, :], ACT.Copy).then_inc(m_hi, 1)
                    if k in POOLED_SPLIT:
                        g = POOLED_SPLIT.index(k)
                        act.wait_ge(pl_f, c * NG + g + 1)
                        if g >= 1:
                            act.wait_ge(pm_ok, c * NG + g)
                        act.activation(pool2[:, 0, :], pooled[:, :], ACT.Copy).then_inc(pl_hi, 1)
                    if k in POOL_GATE_SPLIT:
                        g = POOL_GATE_SPLIT.index(k)
                        act.wait_ge(gated_p, c * NG + g + 1)
                        act.activation(gpl[:, 0, g, :], gated_pool[:, :], ACT.Copy).then_inc(gp_hi, 1)
                    if k == CARRY:
                        act.wait_ge(pl_f, c * NG + NG)
                        act.activation(u[:, :, 0:HIST], u[:, :, T:HIST + T], ACT.Copy).then_inc(carried, 1)
                    if k in H_SPLIT:
                        quarter = H_SPLIT.index(k)
                        h_high(c * 2 + 2 + quarter // 2, quarter)
                    for s in range(4):
                        if SQUARES[s] == k:
                            act.wait_ge(w_ok, c * NW + 3)
                            if s >= 1:
                                act.wait_ge(ss_ok, c * 4 + s)
                            act.activation(junk, y[:, s, :].rearrange("p (g d) -> p g d", g=NG), ACT.Square,
                                           accum_out=fstat[:, s, 0:1]).then_inc(ss_ok, 1)
            act.wait_ge(y_add, KD * NC)
            for s in range(4):
                act.wait_ge(ss_ok, NC * 4 + s)
                act.activation(junk, y[:, s, :].rearrange("p (g d) -> p g d", g=NG), ACT.Square,
                               accum_out=fstat[:, s, 0:1]).then_inc(ss_ok, 1)

        @block.gpsimd
        def _(pool):
            pool.memset(half[:, :], -0.5).then_inc(win_step, 1)
            pool.memset(y[:, :, :], 0.0).then_inc(y_zero, 1)
            pool.wait_ge(const_in, CONSTS)
            pool.wait_ge(win_step, 1)

            def rms(count, s):
                wait_all(pool, const_in, CONSTS, (ss_ok, count + 1))
                pool.tensor_scalar(fstat[:, s, 1:2], fstat[:, s, 0:1], 1.0 / D, EPS, ALU.mult, ALU.add).then_inc(fvar_ok, 1)
                wait_all(pool, const_in, CONSTS, (fvar_ok, count + 1))
                pool.tensor_tensor(fstat[:, s, 2:3], fstat[:, s, 1:2], half[:, :], ALU.pow).then_inc(rinv_ok, 1)

            with pool.Fori(0, NC) as c:
                done = [0]

                def own(instruction):
                    done[0] += 1
                    instruction.then_inc(win_step, 1)
                    wait_all(pool, const_in, CONSTS, (win_step, c * win_steps + done[0] + 1))

                for g in range(NG):
                    wait_all(pool, const_in, CONSTS, (u_sb, c * NG + g + 1), *([(pl_f, c * NG + g - 1)] if g > 1 else []))
                    source, start = u[:, g, :], 0
                    for level in range(levels[g]):
                        shift = 1 << level
                        start += shift
                        out = win[g % 2 * 2 + level % 2]
                        own(pool.tensor_tensor(out[:, start:HIST + T], source[:, start:HIST + T],
                                               source[:, start - shift:HIST + T - shift], ALU.add))
                        source = out
                    sums = source
                    own(pool.tensor_tensor(sums[:, HIST:2 * HIST], sums[:, HIST:2 * HIST], head[:, g, :], ALU.mult))
                    if g == 0:
                        wait_all(pool, const_in, CONSTS, (pick_in, c * 16 + 16))
                    d = slice(HIST + LAST, HIST + LAST + NDEC)
                    own(pool.tensor_tensor(t1[:, :], hsum[:, g, :], u[:, g, d], ALU.add))
                    own(pool.tensor_tensor(t2[:, :], t1[:, :], pick[:, 0, :], ALU.mult))
                    own(pool.tensor_tensor(t3[:, :], sums[:, d], pick[:, 1, :], ALU.mult))
                    pool.tensor_tensor(sums[:, d], t2[:, :], t3[:, :], ALU.add).then_inc(sum_ok, 1)
                    wait_all(pool, const_in, CONSTS, (sum_ok, c * NG + g + 1))
                    rms(c * 4 + g, g)
                assert done[0] == win_steps, (done[0], win_steps)
                pool.wait_ge(const_in, CONSTS)
                pool.memset(head[:, :, :], 1.0).then_inc(head_ok, 1)
                for h in range(NH):
                    wait_all(pool, const_in, CONSTS, (ol_hi, c * NH + h + 1),
                             (ol_ok, c * NH + h) if h else (head_ok, c + 1))
                    split(pool, ols[h % 2][:, 1, :], olf[h % 2][:, :], ols[h % 2][:, 0, :]).then_inc(ol_ok, 1)
            for s in range(4):
                rms(NC * 4 + s, s)

        @block.vector
        def _(dve):
            def weights_low(c, k):
                wait_all(dve, const_in, CONSTS, (w_hi, c * NW + k + 1))
                split(dve, wr[k % 2][:, 1, :, :], ws[k % 4][:, :, :], wr[k % 2][:, 0, :, :]).then_inc(w_ok, 1)

            def h_low(count, quarter):
                wait_all(dve, const_in, CONSTS, (h_hi, count))
                split(dve, ht[:, 1, 2 * quarter:2 * quarter + 2, :], hf[quarter % 2][:, :, :],
                      ht[:, 0, 2 * quarter:2 * quarter + 2, :]).then_inc(h_ok, 1)

            for n in range(2):
                dve.wait_ge(h_hi, n + 1)
                split(dve, ht[:, 1, 2 * n:2 * n + 2, :], hf[n][:, :, :], ht[:, 0, 2 * n:2 * n + 2, :]).then_inc(h_ok, 1)
            for n in range(2):
                dve.wait_ge(w_hi, n + 1)
                split(dve, wr[n][:, 1, :, :], ws[n][:, :, :], wr[n][:, 0, :, :]).then_inc(w_ok, 1)
            for n in range(2, 4):
                dve.wait_ge(h_hi, n + 1)
                split(dve, ht[:, 1, 2 * n:2 * n + 2, :], hf[n % 2][:, :, :],
                      ht[:, 0, 2 * n:2 * n + 2, :]).then_inc(h_ok, 1)
            dve.wait_ge(small_hi, 1)
            split(dve, wuv[:, 1, :, :].rearrange("p (g h) v -> p g (h v)", g=NG), wuv_f,
                  wuv[:, 0, :, :].rearrange("p (g h) v -> p g (h v)", g=NG))
            split(dve, wpl[:, 1, :, :], wpl_f, wpl[:, 0, :, :])
            dve.wait_ge(const_in, CONSTS)
            for g, w in enumerate(WINDOWS):
                dve.tensor_reduce(hsum[:, g, :],
                                  hist[:, g, :].rearrange("p (n h) -> p n h", n=NDEC)[:, :, HIST - (w - 1):HIST],
                                  AX.X, ALU.add)
            dve.memset(u[:, :, 0:HIST], 0.0).then_inc(small_ok, 1)

            def zslot(kind, n):
                return n if kind == "ZP" else n % 3

            with dve.Fori(0, NC) as c:
                def add_output(n):
                    wait_all(dve, const_in, CONSTS, (xt_ok, c * KD + n + 1), (x_in, c * 16 + 16))
                    dve.tensor_tensor(y[:, :, n * P:n * P + P], y[:, :, n * P:n * P + P],
                                      bank[xt_bank(n)][0:SUB, :].rearrange("p (s d) -> p s d", s=4),
                                      ALU.add).then_inc(y_add, 1)

                for k, (kind, n) in enumerate(ORDER):
                    product = bank[out_bank(kind, n)][:, 0:T]
                    wait_all(dve, const_in, CONSTS, (tile_ok, c * NW + k + 1))
                    if kind == "WO" and n >= 2:
                        add_output(n - 2)
                    if k != OP_STEPS[-1]:
                        weights_low(c, k + 2)
                    if k in POOL_GATE:
                        g = POOL_GATE.index(k)
                        wait_all(dve, const_in, CONSTS, (silu_ok, c * (NG + NH) + g + 1),
                                 *([(gp_lo, c * NG + g)] if g else []))
                        dve.scalar_tensor_tensor(gated_pool[:, :], bank[pm_bank(g)][:, 0:T], pscale[:, g:g + 1],
                                                 zs[:, g, :], ALU.mult, ALU.mult).then_inc(gated_p, 1)
                    if k - 1 in [AT["ZA", h] for h in range(NH)]:
                        h = k - 1 - AT["ZA", 0]
                        wait_all(dve, const_in, CONSTS, (gated_hi, c * NH + h + 1))
                        split(dve, gat[:, 1, h, :], gated[:, :], gat[:, 0, h, :]).then_inc(gated_lo, 1)
                    if kind in ("ZP", "ZA"):
                        z = n if kind == "ZP" else NG + n
                        wait_all(dve, const_in, CONSTS, (sig_ok, c * (NG + NH) + z + 1))
                        dve.tensor_tensor(zs[:, zslot(kind, n), :], product, sig[:, :], ALU.mult).then_inc(silu_ok, 1)
                    if kind == "ZA":
                        wait_all(dve, const_in, CONSTS, (silu_ok, c * (NG + NH) + z + 1),
                                 *([(gated_lo, c * NH + n)] if n else []))
                        dve.tensor_tensor(gated[:, :], bank[o_bank(n)][:, 0:T], zs[:, zslot(kind, n), :],
                                          ALU.mult).then_inc(gated_ok, 1)
                    if kind == "OA":
                        wait_all(dve, const_in, CONSTS, (sa_ok, c * KD + n + 1))
                        dve.tensor_tensor(ya[n % 2][:, :], product, sig[:, :], ALU.mult).then_inc(ya_ok, 1)
                    if kind == "OP":
                        wait_all(dve, const_in, CONSTS, (sp_ok, c * KD + n + 2))
                        for a in range(2):
                            dve.tensor_tensor(gate_p[a][:, :], bank[6 + a][:, 0:T], gate_p[a][:, :],
                                              ALU.mult).then_inc(yp_ok, 1)
                        for a in range(2):
                            wait_all(dve, const_in, CONSTS, (yp_ok, c * KD + n + a + 1), (ya_ok, c * KD + n + a + 1))
                            dve.tensor_tensor(ya[a][:, :], ya[a][:, :], gate_p[a][:, :], ALU.add).then_inc(m_ok, 1)
                        for a in range(2):
                            wait_all(dve, const_in, CONSTS, (m_hi, c * KD + n + a + 1), (m_ok, c * KD + n + a + 1))
                            split(dve, mrg[:, 1, n + a, :], ya[a][:, :], mrg[:, 0, n + a, :]).then_inc(m_lo, 1)
                    if k == OP_STEPS[-1]:
                        weights_low(c, k + 2)
                    if k in POOLED:
                        g = POOLED.index(k)
                        wait_all(dve, const_in, CONSTS, (sum_ok, c * NG + g + 1),
                                 *([(pl_ok, c * NG + g)] if g else []))
                        dve.scalar_tensor_tensor(pooled[:, :], win[g % 2 * 2 + (levels[g] - 1) % 2][:, HIST:HIST + T],
                                                 1.0 / WINDOWS[g], u[:, g, HIST:HIST + T], ALU.mult,
                                                 ALU.subtract).then_inc(pl_f, 1)
                    if k in POOLED_SPLIT:
                        g = POOLED_SPLIT.index(k)
                        wait_all(dve, const_in, CONSTS, (pl_hi, c * NG + g + 1))
                        split(dve, pool2[:, 1, :], pooled[:, :], pool2[:, 0, :]).then_inc(pl_ok, 1)
                    if k in POOL_GATE_SPLIT:
                        g = POOL_GATE_SPLIT.index(k)
                        wait_all(dve, const_in, CONSTS, (gp_hi, c * NG + g + 1))
                        split(dve, gpl[:, 1, g, :], gated_pool[:, :], gpl[:, 0, g, :]).then_inc(gp_lo, 1)
                    if k in H_SPLIT:
                        quarter = H_SPLIT.index(k)
                        h_low(c * 4 + 5 + quarter, quarter)
                    if k in FINAL:
                        s = FINAL.index(k)
                        wait_all(dve, const_in, CONSTS, (rinv_ok, c * 4 + s + 1))
                        dve.scalar_tensor_tensor(y[:, s, :], y[:, s, :], fstat[:, s, 2:3], gfin[:, :], ALU.mult,
                                                 ALU.mult).then_inc(y_ok, 1)
                add_output(KD - 2)
                add_output(KD - 1)
            for s in range(4):
                dve.wait_ge(rinv_ok, NC * 4 + s + 1)
                dve.scalar_tensor_tensor(y[:, s, :], y[:, s, :], fstat[:, s, 2:3], gfin[:, :], ALU.mult,
                                         ALU.mult).then_inc(y_ok, 1)

        @block.tensor
        def _(pe):
            def turn_output(c, n):
                pe.wait_ge(yt_sb, c * KD + n + 1)
                if n >= 2:
                    pe.wait_ge(y_add, c * KD + n - 1)
                for s in range(4):
                    mm = pe.transpose(bank[xt_bank(n)][0:SUB, s * P:s * P + P], yt[n % 2][:, s * SUB:s * SUB + SUB],
                                      ident[:, :])
                mm.then_inc(xt_ok, 1)

            with pe.Fori(0, NC) as c:
                for k, (kind, n) in enumerate(ORDER):
                    if k == AT["ZP", 0]:
                        pe.wait_ge(small_ok, 1)
                    if kind == "ZA":
                        h = n
                        pe.wait_ge(ol_ok, c * NH + h + 1)
                        if h >= 2:
                            pe.wait_ge(gated_ok, c * NH + h - 1)
                        three_products(pe, bank[o_bank(h)][:, 0:T], lambda a, _: wuv[:, a, h, :],
                                       lambda b, _: ols[h % 2][:, b, :], 1)
                        pe.wait_ge(silu_ok, c * (NG + NH) + h + 3)
                    pe.wait_ge(w_ok, c * NW + k + 1)
                    if k == 0:
                        pe.wait_ge(h_ok, c * 4 + 4)
                    if kind in ("GA", "GP") and n == 0:
                        pe.wait_ge(gated_ok, c * NH + NH - (kind == "GA"))
                    if kind == "OA" and n == 0:
                        pe.wait_ge(gated_lo, c * NH + NH)
                    if kind == "OP" and n == 0:
                        pe.wait_ge(gp_lo, c * NG + NG)
                    if kind == "WO" and n >= 2:
                        pe.wait_ge(yt_sb, c * KD + n - 1)
                    w = wr[k % 2]
                    if kind == "OP":
                        for a in range(2):
                            mm = three_products(pe, bank[6 + a][:, 0:T], lambda part, j: w[:, part, NG * a + j, :],
                                                lambda part, j: gpl[:, part, j, :], NG)
                    else:
                        moving = {"OA": gat, "WO": mrg}.get(kind, ht)
                        done = 0
                        if kind == "WO" and n == 0:
                            done = KD - 2
                            three_products(pe, bank[out_bank(kind, n)][:, 0:T], lambda part, j: w[:, part, j, :],
                                           lambda part, j: moving[:, part, j, :], done, last=False)
                            pe.wait_ge(m_lo, c * KD + KD)
                        mm = three_products(pe, bank[out_bank(kind, n)][:, 0:T],
                                            lambda part, j: w[:, part, done + j, :],
                                            lambda part, j: moving[:, part, done + j, :], KD - done, first=done == 0)
                    mm.then_inc(tile_ok, 1)
                    if k in POOL_MM:
                        g = POOL_MM.index(k)
                        pe.wait_ge(pl_ok, c * NG + g + 1)
                        three_products(pe, bank[pm_bank(g)][:, 0:T], lambda a, _: wpl[:, a, g, :],
                                       lambda b, _: pool2[:, b, :], 1).then_inc(pm_ok, 1)
                    if kind == "WO" and n >= 1:
                        turn_output(c, n - 1)
                turn_output(c, KD - 1)


def finish(outs):
    y = outs["y"][T:]
    tail = outs["u_tail"].transpose(2, 1, 0).reshape(TAIL, NG * P)
    state = np.concatenate([outs["hist_out"], tail[HIST:, None, :]], axis=1)
    return (y[None, :SEQ], y[SEQ:SEQ + NDEC, None], outs["ckv"][None, None, :SEQ], outs["krope"][None, None, :SEQ],
            tail[None, None, :HIST], outs["ckv"][None, SEQ:SEQ + NDEC, None],
            outs["krope"][None, SEQ:SEQ + NDEC, None], state[None])


def build(nc, io):
    with ExitStack() as ctx:
        def sb(name, shape, dt=f32):
            return ctx.enter_context(nc.sbuf_tensor(name, shape, dt))

        keep = {
            "ident": sb("ident", [P, P]),
            "mask": sb("mask", [P, 512]),
            "kt": sb("kt", [P, NT, 4, P], f32r),
            "kv": sb("kv", [P, NT, 2, R], f32r),
        }
        project(nc, io, keep)
        early = early_decode(nc, ctx)
        attend(nc, io, keep, early)
        decode(nc, io, keep, early)
    merge(nc, io)


INPUTS = ("x", "w_lat", "w_uq_t", "w_uk_t", "w_uq_rope", "g_pre", "g_kv", "g_q", "cos", "sin", "mask", "ident",
          "w", "w_uv", "w_pool", "pool_scale", "head", "hist", "hist_t", "pick", "g_final",
          "pages", "page_part", "own", "cache_ckv", "cache_krope")
OUTPUTS = {"ckv": (ROWS, R), "krope": (ROWS, ROPE), "y": ((NC + 1) * T, D), "u_tail": (P, NG, TAIL),
           "hist_out": (NDEC, HIST - 1, NG * P)}
SCRATCH = {"olat": (P, NH, TOK), "ht": (P, KD, ROWS), "q": (NT, P, NH + NH // 2, P)}


def laid_out(x_prompt, x_sample, cache_ckv, cache_krope, state_pool, page_table, g_pre, w_in, g_q, w_uq,
             g_kv, w_uk, w_uv, w_o_att, w_pool, pool_scale, w_o_pool, w_out, g_final):
    c = np.ascontiguousarray
    w_in, w_uq, w_uk, w_uv = w_in[0], w_uq[0].reshape(QR, NH, NOPE + ROPE), w_uk[0], w_uv[0]
    x = np.zeros((ROWS, D), np.float32)
    x[:SEQ] = x_prompt[0]
    x[SEQ:SEQ + NDEC] = x_sample[:, 0]
    inv = (10000.0 ** (-np.arange(ROPE // 2) / (ROPE // 2))).astype(np.float32)
    pos = np.minimum(np.arange(ROWS), PAST).astype(np.float32)
    angle = np.tile(pos[:, None] * inv[None, :], (1, 2))
    by_tile = lambda a: c(a.reshape(NT, P, ROPE).transpose(1, 0, 2))
    mask = np.zeros((P, 512), np.float32)
    mask[:, 384:][np.arange(P)[None, :] > np.arange(P)[:, None]] = NEG
    rows = lambda a, k: c(a.reshape(k, P, -1).transpose(1, 0, 2))
    za = LAT
    up = za + NH * P
    zp = up + NG * P
    ga = zp + NG * P
    sources = {"ZA": w_in[:, za:up], "U": w_in[:, up:zp], "ZP": w_in[:, zp:ga], "GA": w_in[:, ga:ga + D],
               "GP": w_in[:, ga + D:], "OA": w_o_att[0], "WO": w_out[0]}
    w = np.empty((NW, P, KD, P), np.float32)
    for k, (kind, n) in enumerate(ORDER):
        if kind == "OP":
            for a in range(2):
                w[k, :, NG * a:NG * a + NG] = rows(w_o_pool[0][:, (n + a) * P:(n + a + 1) * P], NG)
        else:
            w[k] = rows(sources[kind][:, n * P:n * P + P], KD)
    count = np.minimum(np.array(WINDOWS)[:, None], np.arange(HIST)[None, :] + 1)
    head = np.broadcast_to((np.array(WINDOWS)[:, None] / count).astype(np.float32), (P, NG, HIST))
    own = np.full((NDEC, NH, NDEC), NEG, np.float32)
    own[np.arange(NDEC), :, np.arange(NDEC)] = 0
    own = own.reshape(NDEC * NH, NDEC)
    pick = np.zeros((NC, P, 2, NDEC), np.float32)
    pick[NC - 1, :, 0], pick[:NC - 1, :, 1] = 1, 1
    return {
        "x": x,
        "w_lat": rows(w_in[:, :LAT], KD),
        "w_uq_t": c(w_uq[:, :, :NOPE].transpose(2, 1, 0)),
        "w_uk_t": c(w_uk.transpose(2, 1, 0)),
        "w_uq_rope": rows(w_uq[:, :, NOPE:].reshape(QR, QROPE), KQ),
        "g_pre": c(g_pre[0]), "g_kv": c(g_kv[0]),
        "g_q": c(g_q[0].reshape(KQ, P).T),
        "cos": by_tile(np.cos(angle)), "sin": by_tile(np.sin(angle)),
        "mask": mask, "ident": np.eye(P, dtype=np.float32),
        "w": w.reshape(NW, P, KD * P),
        "w_uv": c(w_uv.reshape(R, NG, 2 * P)),
        "w_pool": c(w_pool[0].transpose(1, 0, 2)),
        "pool_scale": c(pool_scale[0].reshape(NG, P).T),
        "head": c(head), "pick": pick,
        "hist": c(state_pool[0]),
        "hist_t": c(state_pool[0].reshape(NDEC, HIST, NG, P).transpose(3, 2, 0, 1).reshape(P, NG, NDEC * HIST)),
        "g_final": c(g_final),
        "pages": c(np.repeat(page_table.T.astype(np.int32, copy=False), P // NPAGES, axis=0)),
        "page_part": c(np.broadcast_to((np.arange(P) % (P // NPAGES))[:, None], (P, NDEC)).astype(np.int32)),
        "own": own,
        "cache_ckv": c(cache_ckv[0].reshape(NPHYS * P // NPAGES, -1)),
        "cache_krope": c(cache_krope[0].reshape(NPHYS * P // NPAGES, -1)),
    }


def kernel(**inputs):
    import concourse.bacc as bacc
    from concourse.bass_utils import run_bass_kernel_spmd

    arrays = laid_out(**{name: np.asarray(array) for name, array in inputs.items()})
    nc = bacc.Bacc("TRN2", target_bir_lowering=False, num_devices=1)
    io = {name: nc.dram_tensor("in_" + name, arrays[name].shape, mybir.dt.from_np(arrays[name].dtype),
                               kind="ExternalInput").ap() for name in INPUTS}
    for shapes, kind in ((OUTPUTS, "ExternalOutput"), (SCRATCH, "Internal")):
        for name, shape in shapes.items():
            io[name] = nc.dram_tensor("out_" + name, shape, f32, kind=kind).ap()
    build(nc, io)
    if not nc.is_finalized():
        nc.finalize()
    result = run_bass_kernel_spmd(nc, [{"in_" + name: arrays[name] for name in INPUTS}], core_ids=[0]).results[0]
    return finish({name: result["out_" + name] for name in OUTPUTS})
```
